# Optimizing a Trainium2 kernel written in Bass

```python
import math
import jax, jax.numpy as jnp
from jax import lax
import numpy as np

D_MODEL = 1024
BATCH = 1
SEQ = 256
DEPTH = 2

CHUNK = 64
Q_BLOCK = 128
N_A_LAYERS = DEPTH // 2
N_B_LAYERS = DEPTH - N_A_LAYERS
DIFF_HEADS = 8
DIFF_HEAD_DIM = D_MODEL // (2 * DIFF_HEADS)
DIFF_V_DIM = 2 * DIFF_HEAD_DIM
SB_HEADS = 16
SB_HEAD_DIM = D_MODEL // SB_HEADS
PEER_HEADS = 8
PEER_N_KEYS = 128
PEER_N_EXPERTS = PEER_N_KEYS * PEER_N_KEYS
PEER_TOPK = 16
PEER_QUERY_DIM = 128
PEER_HALF = PEER_QUERY_DIM // 2
PEER_TOKEN_BLOCK = 128
ROPE_THETA = 10000.0
LN_EPS = 1e-5
RMS_EPS = 1e-5
DEEPNORM_ALPHA = (2.0 * DEPTH) ** 0.25
DEEPNORM_BETA = (8.0 * DEPTH) ** -0.25


def _layer_norm(x, g, b):
    xf = x.astype(jnp.float32)
    mu = jnp.mean(xf, axis=-1, keepdims=True)
    var = jnp.mean(jnp.square(xf - mu), axis=-1, keepdims=True)
    y = (xf - mu) * lax.rsqrt(var + LN_EPS)
    return (y * g.astype(jnp.float32) + b.astype(jnp.float32)).astype(x.dtype)

def _rope_tables(seq):
    pos = jnp.arange(seq, dtype=jnp.float32)
    inv = ROPE_THETA ** (-jnp.arange(0, DIFF_HEAD_DIM, 2, dtype=jnp.float32) / DIFF_HEAD_DIM)
    ang = pos[:, None] * inv[None, :]
    ang = jnp.concatenate([ang, ang], axis=-1)
    return jnp.cos(ang), jnp.sin(ang)

def _rope(t, cos, sin):
    half = t.shape[-1] // 2
    rot = jnp.concatenate([-t[..., half:], t[..., :half]], axis=-1)
    return (t * cos[None, :, None, :] + rot * sin[None, :, None, :]).astype(t.dtype)

def _diff_attention(x, w_qkv, w_o, lam_params, subln_g, lambda_init, cos, sin):
    B, S, D = x.shape
    nb = S // Q_BLOCK
    qkv = x @ w_qkv
    q, k, v = qkv[..., :D], qkv[..., D:2 * D], qkv[..., 2 * D:]
    q = _rope(q.reshape(B, S, 2 * DIFF_HEADS, DIFF_HEAD_DIM), cos, sin)
    k = _rope(k.reshape(B, S, 2 * DIFF_HEADS, DIFF_HEAD_DIM), cos, sin)
    v = v.reshape(B, S, DIFF_HEADS, DIFF_V_DIM)
    kh = k.reshape(B, S, DIFF_HEADS, 2, DIFF_HEAD_DIM).transpose(0, 2, 3, 1, 4)
    vh = v.transpose(0, 2, 1, 3)
    qb = q.reshape(B, nb, Q_BLOCK, DIFF_HEADS, 2, DIFF_HEAD_DIM).transpose(1, 0, 3, 4, 2, 5)
    lp = lam_params.astype(jnp.float32)
    lam = jnp.exp(jnp.sum(lp[0] * lp[1])) - jnp.exp(jnp.sum(lp[2] * lp[3])) + lambda_init
    key_chunk = jnp.arange(S) // CHUNK
    scale = DIFF_HEAD_DIM ** -0.5

    def block(args):
        qblk, i = args
        t = i * Q_BLOCK + jnp.arange(Q_BLOCK)
        mask = key_chunk[None, :] <= (t // CHUNK)[:, None]
        s = jnp.einsum('bhmqd,bhmkd->bhmqk', qblk, kh).astype(jnp.float32) * scale
        p = jax.nn.softmax(jnp.where(mask, s, -jnp.inf), axis=-1)
        a = p[:, :, 0] - lam * p[:, :, 1]
        return jnp.einsum('bhqk,bhkd->bhqd', a.astype(vh.dtype), vh)

    o = lax.map(block, (qb, jnp.arange(nb)))
    of = o.astype(jnp.float32)
    of = of * lax.rsqrt(jnp.mean(of * of, axis=-1, keepdims=True) + RMS_EPS)
    of = of * subln_g.astype(jnp.float32) * (1.0 - lambda_init)
    o = of.astype(x.dtype).transpose(1, 0, 3, 2, 4).reshape(B, S, DIFF_HEADS * DIFF_V_DIM)
    return o @ w_o

def _shared_kv(x, w_kv):
    B, S, D = x.shape
    kv = x @ w_kv
    k = kv[..., :D].reshape(B, S, SB_HEADS, SB_HEAD_DIM).transpose(0, 2, 1, 3)
    v = kv[..., D:].reshape(B, S, SB_HEADS, SB_HEAD_DIM).transpose(0, 2, 1, 3)
    return k, v

def _stick_breaking(x, w_q, w_o, k_sb, v_sb):
    B, S, D = x.shape
    nb = S // Q_BLOCK
    q = (x @ w_q).reshape(B, nb, Q_BLOCK, SB_HEADS, SB_HEAD_DIM).transpose(1, 0, 3, 2, 4)
    key_pos = jnp.arange(S)
    scale = SB_HEAD_DIM ** -0.5

    def block(args):
        qblk, i = args
        t = i * Q_BLOCK + jnp.arange(Q_BLOCK)
        mask = key_pos[None, :] < t[:, None]
        z = jnp.einsum('bhqd,bhkd->bhqk', qblk, k_sb).astype(jnp.float32) * scale
        log_one_minus = jnp.where(mask, jax.nn.log_sigmoid(-z), 0.0)
        tail = lax.cumsum(log_one_minus, axis=3, reverse=True) - log_one_minus
        a = jnp.where(mask, jnp.exp(jax.nn.log_sigmoid(z) + tail), 0.0)
        return jnp.einsum('bhqk,bhkd->bhqd', a.astype(v_sb.dtype), v_sb)

    o = lax.map(block, (q, jnp.arange(nb)))
    o = o.transpose(1, 0, 3, 2, 4).reshape(B, S, SB_HEADS * SB_HEAD_DIM)
    return o @ w_o

def _peer(x, w_pq, sub_keys, u, v):
    B, S, D = x.shape
    T = B * S
    xt = x.reshape(T, D)
    q = (xt @ w_pq).reshape(T, PEER_HEADS, 2, PEER_HALF)
    scores = jnp.einsum('thcd,hckd->thck', q, sub_keys).astype(jnp.float32)
    s_top, i_top = lax.top_k(scores, PEER_TOPK)
    cand = s_top[:, :, 0, :, None] + s_top[:, :, 1, None, :]
    cand_ids = i_top[:, :, 0, :, None] * PEER_N_KEYS + i_top[:, :, 1, None, :]
    g_s, g_i = lax.top_k(cand.reshape(T, PEER_HEADS, PEER_TOPK * PEER_TOPK), PEER_TOPK)
    expert_ids = jnp.take_along_axis(cand_ids.reshape(T, PEER_HEADS, PEER_TOPK * PEER_TOPK), g_i, axis=-1)
    gates = jax.nn.softmax(g_s, axis=-1).astype(x.dtype)
    nblk = T // PEER_TOKEN_BLOCK
    n_sel = PEER_HEADS * PEER_TOPK
    ids_b = expert_ids.reshape(nblk, PEER_TOKEN_BLOCK, n_sel)
    g_b = gates.reshape(nblk, PEER_TOKEN_BLOCK, n_sel)
    x_b = xt.reshape(nblk, PEER_TOKEN_BLOCK, D)

    def block(args):
        xblk, idb, gb = args
        u_sel = jnp.take(u, idb, axis=0)
        h = jax.nn.gelu(jnp.einsum('td,ted->te', xblk, u_sel), approximate=False)
        v_sel = jnp.take(v, idb, axis=0)
        return jnp.einsum('te,ted->td', gb * h, v_sel)

    out = lax.map(block, (x_b, ids_b, g_b))
    return out.reshape(B, S, D)

def first_inputs(seed: int = 0) -> dict:
    key = jax.random.key(seed)
    ks = jax.random.split(key, 16)
    D = D_MODEL
    f32 = jnp.float32
    nrm = lambda k, shape, s: jax.random.normal(k, shape, f32) * s
    v_col_scale = jnp.concatenate([jnp.ones((2 * D,), f32), jnp.full((D,), DEEPNORM_BETA, f32)])
    kv_col_scale = jnp.concatenate([jnp.ones((D,), f32), jnp.full((D,), DEEPNORM_BETA, f32)])
    return {
        "x": nrm(ks[0], (BATCH, SEQ, D), 1.0),
        "ln_g": 1.0 + nrm(ks[1], (DEPTH, 2, D), 0.02),
        "ln_b": nrm(ks[2], (DEPTH, 2, D), 0.02),
        "w_qkv_a": nrm(ks[3], (N_A_LAYERS, D, 3 * D), D ** -0.5) * v_col_scale,
        "w_o_a": nrm(ks[4], (N_A_LAYERS, DIFF_HEADS * DIFF_V_DIM, D), D ** -0.5 * DEEPNORM_BETA),
        "lambda_qk_a": nrm(ks[5], (N_A_LAYERS, 4, DIFF_HEAD_DIM), 0.1),
        "subln_g_a": 1.0 + nrm(ks[6], (N_A_LAYERS, DIFF_V_DIM), 0.02),
        "w_kv_b": nrm(ks[7], (D, 2 * D), D ** -0.5) * kv_col_scale,
        "w_q_b": nrm(ks[8], (N_B_LAYERS, D, SB_HEADS * SB_HEAD_DIM), D ** -0.5),
        "w_o_b": nrm(ks[9], (N_B_LAYERS, SB_HEADS * SB_HEAD_DIM, D), D ** -0.5 * DEEPNORM_BETA),
        "peer_w_q": nrm(ks[10], (DEPTH, D, PEER_HEADS * PEER_QUERY_DIM), D ** -0.5),
        "peer_sub_keys": nrm(ks[11], (DEPTH, PEER_HEADS, 2, PEER_N_KEYS, PEER_HALF), PEER_HALF ** -0.5),
        "peer_u": nrm(ks[12], (DEPTH, PEER_N_EXPERTS, D), D ** -0.5),
        "peer_v": nrm(ks[13], (DEPTH, PEER_N_EXPERTS, D), DEEPNORM_BETA * PEER_HEADS ** -0.5),
    }

def first_block(x, ln_g, ln_b, w_qkv_a, w_o_a, lambda_qk_a, subln_g_a, w_kv_b, w_q_b, w_o_b,
              peer_w_q, peer_sub_keys, peer_u, peer_v):
    S = x.shape[1]
    cos, sin = _rope_tables(S)
    k_sb = None
    v_sb = None
    for layer in range(DEPTH):
        if layer < N_A_LAYERS:
            lambda_init = 0.8 - 0.6 * math.exp(-0.3 * layer)
            mix = _diff_attention(x, w_qkv_a[layer], w_o_a[layer], lambda_qk_a[layer],
                                  subln_g_a[layer], lambda_init, cos, sin)
        else:
            if layer == N_A_LAYERS:
                k_sb, v_sb = _shared_kv(x, w_kv_b)
            j = layer - N_A_LAYERS
            mix = _stick_breaking(x, w_q_b[j], w_o_b[j], k_sb, v_sb)
        x = _layer_norm(DEEPNORM_ALPHA * x + mix, ln_g[layer, 0], ln_b[layer, 0])
        ffn = _peer(x, peer_w_q[layer], peer_sub_keys[layer], peer_u[layer], peer_v[layer])
        x = _layer_norm(DEEPNORM_ALPHA * x + ffn, ln_g[layer, 1], ln_b[layer, 1])
    return x


N_A_LAYERS_2 = DEPTH // 2
N_B_LAYERS_2 = DEPTH - N_A_LAYERS_2

D_FF = 2816
RMS_EPS_2 = 1e-6

RWKV_HEAD = 64
RWKV_HEADS = D_MODEL // RWKV_HEAD
DECAY_LORA = 64
AAA_LORA = 64
GATE_LORA = 128
GN_EPS = 64e-5

ATT_HEAD = 64
Q_HEADS = D_MODEL // ATT_HEAD
KV_HEADS = 4
GROUP = Q_HEADS // KV_HEADS
WINDOW = 128
BLOCK = 128
KV_WIDTH = KV_HEADS * ATT_HEAD
MASK_VALUE = -1e30


def rms_norm(x, g):
    xf = x.astype(jnp.float32)
    y = xf * lax.rsqrt(jnp.mean(xf * xf, axis=-1, keepdims=True) + RMS_EPS_2)
    return (y * g.astype(jnp.float32)).astype(x.dtype)

def swiglu(x, w_in, w_out):
    gate, up = jnp.split(x @ w_in, 2, axis=-1)
    return (jax.nn.silu(gate) * up) @ w_out

def rwkv7_time_mix(x, mu, w_rkv, w_o, w0, w1, w2, a0, a1, a2, g1, g2,
                   k_k, k_a, r_k, gn_g, gn_b):
    B, T, C = x.shape
    H, N = RWKV_HEADS, RWKV_HEAD
    f32 = jnp.float32
    x_prev = jnp.pad(x, ((0, 0), (1, 0), (0, 0)))[:, :-1]
    xx = x_prev - x
    xr, xw, xk, xv, xa, xg = [x + xx * mu[i] for i in range(6)]

    r = xr @ w_rkv[0]
    k = xk @ w_rkv[1]
    v = xv @ w_rkv[2]
    w = -jax.nn.softplus(-(w0 + jnp.tanh(xw @ w1) @ w2)) - 0.5
    decay = jnp.exp(-jnp.exp(w.astype(f32)))
    a = jax.nn.sigmoid(a0 + (xa @ a1) @ a2)
    g = jax.nn.sigmoid(xg @ g1) @ g2

    heads = lambda t: t.reshape(B, T, H, N).astype(f32)
    kk = heads(k * k_k)
    kk = kk / jnp.maximum(jnp.linalg.norm(kk, axis=-1, keepdims=True), 1e-12)
    k = k * (1.0 + (a - 1.0) * k_a)
    r_h, k_h, v_h, a_h, w_h = heads(r), heads(k), heads(v), heads(a), heads(decay)
    b_h = kk * a_h

    def step(S, inp):
        r_t, w_t, k_t, v_t, kk_t, b_t = inp
        sa = jnp.einsum('bhij,bhj->bhi', S, -kk_t)
        S = (S * w_t[:, :, None, :] + sa[..., None] * b_t[:, :, None, :]
             + v_t[..., None] * k_t[:, :, None, :])
        y = jnp.einsum('bhij,bhj->bhi', S, r_t)
        return S, y

    xs = tuple(jnp.moveaxis(t, 1, 0) for t in (r_h, w_h, k_h, v_h, kk, b_h))
    S0 = jnp.zeros((B, H, N, N), f32)
    _, y = lax.scan(step, S0, xs)
    y = jnp.moveaxis(y, 0, 1)

    mean = jnp.mean(y, axis=-1, keepdims=True)
    var = jnp.mean(jnp.square(y - mean), axis=-1, keepdims=True)
    y = ((y - mean) * lax.rsqrt(var + GN_EPS)).reshape(B, T, C)
    y = y * gn_g.astype(f32) + gn_b.astype(f32)
    bonus = jnp.sum(r_h * k_h * r_k.astype(f32), axis=-1, keepdims=True) * v_h
    y = (y + bonus.reshape(B, T, C)).astype(x.dtype)
    return (y * g) @ w_o

def swa_sinks(xq, k_sh, v_sh, w_q, b_q, w_o, b_o, sinks):
    B, T, _ = xq.shape
    NB = T // BLOCK
    q = (xq @ w_q + b_q).reshape(B, NB, BLOCK, KV_HEADS, GROUP, ATT_HEAD)

    def banded(t):
        t = t.reshape(B, NB, BLOCK, KV_HEADS, ATT_HEAD)
        prev = jnp.pad(t, ((0, 0), (1, 0), (0, 0), (0, 0), (0, 0)))[:, :-1]
        return jnp.concatenate([prev, t], axis=2)

    kb, vb = banded(k_sh), banded(v_sh)
    s = jnp.einsum('bnqkgd,bnskd->bnkgqs', q, kb).astype(jnp.float32) * (ATT_HEAD ** -0.5)
    blk = jnp.arange(NB)[:, None, None] * BLOCK
    q_pos = blk + jnp.arange(BLOCK)[None, :, None]
    k_pos = blk - BLOCK + jnp.arange(2 * BLOCK)[None, None, :]
    valid = (k_pos >= 0) & (k_pos <= q_pos) & (q_pos - k_pos < WINDOW)
    s = jnp.where(valid[None, :, None, None], s, MASK_VALUE)
    sink = jnp.broadcast_to(
        sinks.astype(jnp.float32).reshape(1, 1, KV_HEADS, GROUP, 1, 1), s.shape[:-1] + (1,))
    p = jax.nn.softmax(jnp.concatenate([s, sink], axis=-1), axis=-1)[..., :-1]
    o = jnp.einsum('bnkgqs,bnskd->bnqkgd', p.astype(vb.dtype), vb)
    o = o.reshape(B, T, Q_HEADS * ATT_HEAD)
    return o @ w_o + b_o

def second_inputs(seed: int = 0) -> dict:
    key = jax.random.key(seed)
    ks = iter(jax.random.split(key, 32))
    D, NA, NBL = D_MODEL, N_A_LAYERS_2, N_B_LAYERS_2
    f32 = jnp.float32

    def nrm(shape, scale):
        return scale * jax.random.normal(next(ks), shape, f32)

    def uni(shape, lo, hi):
        return jax.random.uniform(next(ks), shape, f32, lo, hi)

    return {
        "x": nrm((BATCH, SEQ, D), 1.0),
        "norm_g": 1.0 + nrm((DEPTH, 6, D), 0.05),
        "ffn_w_in": nrm((DEPTH, 2, D, 2 * D_FF), D ** -0.5),
        "ffn_w_out": nrm((DEPTH, 2, D_FF, D), D_FF ** -0.5),
        "rwkv_mu": uni((NA, 6, D), 0.0, 1.0),
        "rwkv_w_rkv": nrm((NA, 3, D, D), D ** -0.5),
        "rwkv_w_o": nrm((NA, D, D), D ** -0.5),
        "rwkv_w0": uni((NA, D), -6.0, -1.0),
        "rwkv_w1": nrm((NA, D, DECAY_LORA), D ** -0.5),
        "rwkv_w2": nrm((NA, DECAY_LORA, D), 0.1 * DECAY_LORA ** -0.5),
        "rwkv_a0": nrm((NA, D), 0.1),
        "rwkv_a1": nrm((NA, D, AAA_LORA), D ** -0.5),
        "rwkv_a2": nrm((NA, AAA_LORA, D), 0.1 * AAA_LORA ** -0.5),
        "rwkv_g1": nrm((NA, D, GATE_LORA), D ** -0.5),
        "rwkv_g2": nrm((NA, GATE_LORA, D), GATE_LORA ** -0.5),
        "rwkv_k_k": 0.85 + nrm((NA, D), 0.05),
        "rwkv_k_a": 1.0 + nrm((NA, D), 0.05),
        "rwkv_r_k": nrm((NA, RWKV_HEADS, RWKV_HEAD), 0.1),
        "rwkv_gn_g": 1.0 + nrm((NA, D), 0.05),
        "rwkv_gn_b": nrm((NA, D), 0.02),
        "kv_norm_g": 1.0 + nrm((D,), 0.05),
        "w_kv": nrm((D, 2 * KV_WIDTH), D ** -0.5),
        "b_kv": nrm((2 * KV_WIDTH,), 0.02),
        "attn_w_q": nrm((NBL, D, Q_HEADS * ATT_HEAD), D ** -0.5),
        "attn_b_q": nrm((NBL, Q_HEADS * ATT_HEAD), 0.02),
        "attn_w_o": nrm((NBL, Q_HEADS * ATT_HEAD, D), (Q_HEADS * ATT_HEAD) ** -0.5),
        "attn_b_o": nrm((NBL, D), 0.02),
        "attn_sinks": nrm((NBL, Q_HEADS), 1.0),
    }

def second_block(x, norm_g, ffn_w_in, ffn_w_out,
              rwkv_mu, rwkv_w_rkv, rwkv_w_o, rwkv_w0, rwkv_w1, rwkv_w2,
              rwkv_a0, rwkv_a1, rwkv_a2, rwkv_g1, rwkv_g2, rwkv_k_k, rwkv_k_a,
              rwkv_r_k, rwkv_gn_g, rwkv_gn_b,
              kv_norm_g, w_kv, b_kv,
              attn_w_q, attn_b_q, attn_w_o, attn_b_o, attn_sinks):
    B, T, _ = x.shape
    h = x
    k_sh = v_sh = None
    for layer in range(DEPTH):
        g = norm_g[layer]
        h = h + 0.5 * rms_norm(swiglu(rms_norm(h, g[0]), ffn_w_in[layer, 0], ffn_w_out[layer, 0]), g[1])
        u = rms_norm(h, g[2])
        if layer < N_A_LAYERS_2:
            i = layer
            m = rwkv7_time_mix(u, rwkv_mu[i], rwkv_w_rkv[i], rwkv_w_o[i], rwkv_w0[i],
                               rwkv_w1[i], rwkv_w2[i], rwkv_a0[i], rwkv_a1[i], rwkv_a2[i],
                               rwkv_g1[i], rwkv_g2[i], rwkv_k_k[i], rwkv_k_a[i],
                               rwkv_r_k[i], rwkv_gn_g[i], rwkv_gn_b[i])
        else:
            j = layer - N_A_LAYERS_2
            m = swa_sinks(u, k_sh, v_sh, attn_w_q[j], attn_b_q[j], attn_w_o[j],
                          attn_b_o[j], attn_sinks[j])
        h = h + rms_norm(m, g[3])
        h = h + 0.5 * rms_norm(swiglu(rms_norm(h, g[4]), ffn_w_in[layer, 1], ffn_w_out[layer, 1]), g[5])
        if layer == N_A_LAYERS_2 - 1:
            kv = rms_norm(h, kv_norm_g) @ w_kv + b_kv
            k_sh = kv[..., :KV_WIDTH].reshape(B, T, KV_HEADS, ATT_HEAD)
            v_sh = kv[..., KV_WIDTH:].reshape(B, T, KV_HEADS, ATT_HEAD)
    return h


def setup_inputs(seed=0):
    out = dict(first_inputs(seed))
    for name, value in second_inputs(seed + 1).items():
        if name != "x":
            out[name + "_2"] = value
    return out


def reference(
    x, ln_g, ln_b, w_qkv_a, w_o_a, lambda_qk_a, subln_g_a, w_kv_b, w_q_b, w_o_b, peer_w_q,
    peer_sub_keys, peer_u, peer_v, norm_g_2, ffn_w_in_2, ffn_w_out_2, rwkv_mu_2, rwkv_w_rkv_2,
    rwkv_w_o_2, rwkv_w0_2, rwkv_w1_2, rwkv_w2_2, rwkv_a0_2, rwkv_a1_2, rwkv_a2_2, rwkv_g1_2,
    rwkv_g2_2, rwkv_k_k_2, rwkv_k_a_2, rwkv_r_k_2, rwkv_gn_g_2, rwkv_gn_b_2, kv_norm_g_2,
    w_kv_2, b_kv_2, attn_w_q_2, attn_b_q_2, attn_w_o_2, attn_b_o_2, attn_sinks_2,
):
    x = first_block(
        x, ln_g, ln_b, w_qkv_a, w_o_a, lambda_qk_a, subln_g_a, w_kv_b, w_q_b, w_o_b, peer_w_q,
        peer_sub_keys, peer_u, peer_v,
    )
    return second_block(
        x, norm_g_2, ffn_w_in_2, ffn_w_out_2, rwkv_mu_2, rwkv_w_rkv_2, rwkv_w_o_2, rwkv_w0_2,
        rwkv_w1_2, rwkv_w2_2, rwkv_a0_2, rwkv_a1_2, rwkv_a2_2, rwkv_g1_2, rwkv_g2_2, rwkv_k_k_2,
        rwkv_k_a_2, rwkv_r_k_2, rwkv_gn_g_2, rwkv_gn_b_2, kv_norm_g_2, w_kv_2, b_kv_2,
        attn_w_q_2, attn_b_q_2, attn_w_o_2, attn_b_o_2, attn_sinks_2,
    )


_drawn_inputs = setup_inputs


def setup_inputs(seed=0):
    import zlib

    import numpy as np

    out = dict(_drawn_inputs(seed))
    spreads = {}
    factors = {'subln_g_a': 2.849, 'rwkv_w1_2': 8.0, 'rwkv_w2_2': 8.0, 'attn_b_q_2': 7.433}
    for name, (base, spread) in spreads.items():
        noise = np.random.default_rng([zlib.crc32(name.encode()), seed]).standard_normal(out[name].shape)
        drawn = base * np.exp(spread * noise) if base else spread * noise
        out[name] = __import__('jax').numpy.asarray(drawn.astype(out[name].dtype))
    for name, factor in factors.items():
        out[name] = (out[name] * factor).astype(out[name].dtype)
    return out
```

```python
from contextlib import ExitStack
import math

import numpy as np
import concourse.bass as bass
from concourse import mybir
from concourse.alu_op_type import AluOpType as ALU

ACT = mybir.ActivationFunctionType
AX = mybir.AxisListType.X
F32 = mybir.dt.float32
R32 = mybir.dt.float32r
U32 = mybir.dt.uint32

P = 128
SEQ, D = 256, 1024
TB = SEQ // P
KT = D // P
HALF = 512
DEPTH = 2
ALPHA = (2.0 * DEPTH) ** 0.25
LN_EPS, RMS_EPS, RMS_EPS_2, GN_EPS = 1e-5, 1e-5, 1e-6, 64e-5
HD = 64
DIFF_HEADS, HEADS = 8, 16
LAMBDA_INIT = 0.8 - 0.6 * math.exp(-0.3 * 0)
NKEY, TOPK, PH = 128, 16, 8
D_FF = 2816
FT = D_FF // P
KV_HEADS, GROUP = 4, 4
LEVELS = 7
FLT_MIN = -3.4028234e38

CH = {}
for _name, _n in (("mu", 48), ("w0", 8), ("a0", 8), ("k_k", 8), ("k_a", 8), ("r_k", 8),
                  ("pre", 48), ("kv_g", 8), ("b_k", 4), ("b_q", 8)):
    CH[_name] = (sum(v[1] for v in CH.values()), _n)
N_CH = sum(v[1] for v in CH.values())
SM = {"lambda": (0, 256), "subln": (256, 128), "sinks": (384, 16), "b_v": (400, 256)}
N_SM = 656
ROWS = {}
for _l in range(2):
    for _s in range(2):
        ROWS[f"ln_g{_l}{_s}"] = len(ROWS)
        ROWS[f"ln_b{_l}{_s}"] = len(ROWS)
for _l in range(2):
    for _s in (1, 3, 5):
        ROWS[f"post{_l}{_s}"] = len(ROWS)
for _s in ("gn_g", "gn_b", "b_o"):
    ROWS[_s] = len(ROWS)
CN = {}
for _name, _n in (("cos", 128), ("sin", 128), ("diff_mask", 512), ("sb_keep", 512),
                  ("sb_drop", 512), ("swa_mask", 512), ("gram_mask", 256), ("levels", 128 * LEVELS),
                  ("pair_ones", 128), ("head_ones", 128)):
    CN[_name] = (sum(v[1] for v in CN.values()), _n)
N_CN = sum(v[1] for v in CN.values())


def constants():
    c = np.zeros((P, N_CN), np.float32)

    def put(name, a):
        o, n = CN[name]
        c[:, o:o + n] = np.asarray(a, np.float32).reshape(P, n)

    pos = np.arange(SEQ, dtype=np.float32)
    inv = (np.float32(10000.0) ** (-np.arange(0, HD, 2, dtype=np.float32) / np.float32(HD))).astype(np.float32)
    ang = pos[:, None] * inv[None, :]
    cos, sin = np.cos(ang), np.sin(ang)
    by_part = lambda a: a.reshape(TB, P, -1).transpose(1, 0, 2)
    put("cos", by_part(np.concatenate([cos, cos], 1)))
    put("sin", by_part(np.concatenate([-sin, sin], 1)))
    t, k = np.arange(SEQ)[:, None], np.arange(SEQ)[None, :]
    put("diff_mask", by_part(np.where(k // 64 <= t // 64, 0.0, -1e30)))
    put("sb_keep", by_part(np.where(k < t, 1.0, 0.0)))
    put("sb_drop", by_part(np.where(k < t, 0.0, 1e30)))
    put("swa_mask", by_part(np.where((k <= t) & (t - k < 128), 0.0, -1e30)))
    s, t = np.arange(P)[:, None], np.arange(P)[None, :]
    put("gram_mask", np.concatenate([s < t, s <= t], 1))
    put("levels", np.stack([(s // (2 << l) == t // (2 << l)) & ((s >> l) % 2 == 0) & ((t >> l) % 2 == 1)
                            for l in range(LEVELS)], 1))
    put("pair_ones", s // HD == t // HD)
    ho = np.zeros((P, KT, HEADS))
    for j in range(KT):
        ho[:HD, j, 2 * j] = 1
        ho[HD:, j, 2 * j + 1] = 1
    put("head_ones", ho)
    fixed = np.concatenate([np.eye(P), np.broadcast_to(np.arange(P), (P, P))], 1).astype(np.float32)
    return c, fixed


class Mark:

    def __init__(self, sem, value):
        self.sem, self.value = sem, value


class Line:

    def __init__(self, sem, engine):
        self.sem, self.engine, self.count, self.seen = sem, engine, 0, {}

    def wait(self, *marks):
        for m in marks:
            if m is None or self.seen.get(id(m.sem), 0) >= m.value:
                continue
            self.seen[id(m.sem)] = m.value
            if self.engine:
                self.engine.wait_ge(m.sem, m.value)

    def last(self):
        return Mark(self.sem, self.count) if self.count else None

    def do(self, make, *after, chain=True):
        self.wait(*after)
        if chain:
            self.wait(self.last())
        self.count += 1
        if self.engine:
            make(self.engine).then_inc(self.sem, 1)
        return self.last()

    def run(self, makes, *after):
        self.wait(*after)
        self.count += 1
        if self.engine:
            for make in makes:
                made = make(self.engine)
            made.then_inc(self.sem, 1)
        return self.last()

    def dma(self, out, in_, sem, value, *after):
        self.wait(*after)
        if self.engine:
            self.engine.dma_start(out, in_).then_inc(sem, 16)
        return Mark(sem, value)


class Ring:

    def __init__(self, slots):
        self.slots, self.free, self.n = slots, [()] * len(slots), 0

    def take(self):
        self.at = self.n % len(self.slots)
        self.n += 1
        return self.slots[self.at], self.free[self.at], self.at

    def give(self, at, *marks):
        self.free[at] = marks


def bcast(ap, axis, n):
    a = ap.unsqueeze(axis)
    shape = list(a.shape)
    shape[axis] = n
    return a.broadcast_to(shape)


class Program:
    RAW, SPLIT = 3, 3

    def __init__(self, nc, dram, out, stages, ctx, placed, which=None, engine=None):
        self.nc, self.dram, self.out, self.ctx, self.placed = nc, dram, out, ctx, placed
        self.first_pass = which is None
        self.n_names = 0
        self.pe, self.act, self.dve, self.pool, self.sp = (
            Line(self.sem(n + "_done"), engine if n == which else None)
            for n in ("tensor", "scalar", "vector", "gpsimd", "sync"))
        self.stages = stages
        sb = lambda *a: self.sb(ctx, *a)
        self.resid = sb("resid", [P, TB, D], F32)
        self.xt_hi = sb("xt_hi", [P, KT, SEQ], R32)
        self.xt_lo = sb("xt_lo", [P, KT, SEQ], R32)
        self.fixed = sb("fixed", [P, 2 * P], F32)
        self.ident, self.iota = self.fixed[:, 0:P], self.fixed[:, P:2 * P]
        self.chan = sb("chan", [P, N_CH], F32)
        self.raw = [sb(f"w_raw{i}", [P, D], F32) for i in range(self.RAW)]
        self.hi = [sb(f"w_hi{i}", [P, D], R32) for i in range(self.SPLIT)]
        self.lo = [sb(f"w_lo{i}", [P, D], R32) for i in range(self.SPLIT)]
        self.raw_sem = [self.sem(f"w_raw_loaded{i}") for i in range(self.RAW)]
        self.banks = [self.place(ctx, f"bank{i}", lambda: nc.psum_tensor(f"bank{i}", [P, HALF], F32))
                      for i in range(8)]
        self.pieces = []
        self.prepared = self.used = 0
        self.split_done, self.piece_done = [], []
        self.n_load = 0
        self.bank_free = [()] * 8

    def place(self, ctx, name, make):
        if self.first_pass:
            self.placed[name] = ctx.enter_context(make())
        return self.placed[name]

    def sem(self, name):
        return self.place(self.ctx, name, lambda: self.nc.semaphore(name))

    def sb(self, ctx, name, shape, dt=F32):
        self.n_names += 1
        name = f"{name}_{self.n_names}"
        return self.place(ctx, name, lambda: self.nc.sbuf_tensor(name, shape, dt))

    def load(self, out, in_, *after):
        self.n_load += 1
        return self.pool.dma(out, in_, self.sem(f"load{self.n_load}"), 16, *after)

    def row(self, name, out, *after):
        r = ROWS[name]
        return self.load(out, self.dram["rows"][r:r + 1, :].broadcast_to([P, D]), *after)

    def const(self, ctx, *names):
        got, marks = {}, []
        for name in names:
            o, n = CN[name]
            got[name] = self.sb(ctx, f"c_{name}_{self.n_load}", [P, n], F32)
            marks.append(self.load(got[name][:, :], self.dram["consts"][:, o:o + n]))
        return got, marks

    def ch(self, name, j):
        o = CH[name][0] + j
        return self.chan[:, o:o + 1]

    def join(self):
        lines = (self.pe, self.act, self.dve, self.pool)
        marks = [a.last() for a in lines]
        for a in lines:
            a.wait(*marks)

    def prepare(self):
        n = self.prepared
        self.prepared += 1
        raw, hi, lo = self.raw[n % self.RAW], self.hi[n % self.SPLIT], self.lo[n % self.SPLIT]
        raw_free = self.split_done[n - self.RAW] if n >= self.RAW else ()
        loaded = self.sp.dma(raw[:, :], self.pieces[n][1], self.raw_sem[n % self.RAW],
                             16 * (n // self.RAW + 1), *raw_free)
        slot_free = self.piece_done[n - self.SPLIT] if n >= self.SPLIT else None
        a = self.act.do(lambda e: e.activation(hi[:, :], raw[:, :], ACT.Copy), loaded, slot_free, chain=False)
        d = self.dve.do(lambda e: e.tensor_tensor(lo[:, :], raw[:, :], hi[:, :].bitcast(F32), ALU.subtract),
                        loaded, a, slot_free, chain=False)
        self.split_done.append((a, d))

    def piece(self, name):
        n = self.used
        assert self.pieces[n][0] == name, (self.pieces[n][0], name)
        self.used += 1
        while self.prepared < min(n + self.SPLIT, len(self.pieces)):
            self.prepare()
        return self.hi[n % self.SPLIT], self.lo[n % self.SPLIT], self.split_done[n]

    def used_by(self, mark):
        self.piece_done.append(mark)

    def product_cols(self, name, bank, xh, xl, *after):
        hi, lo, ready = self.piece(name)
        out = self.banks[bank][:, 0:SEQ]
        makes = []
        for k in range(KT):
            wh, wl = hi[:, k * P:(k + 1) * P], lo[:, k * P:(k + 1) * P]
            for w, x in ((wh, xh), (wh, xl), (wl, xh)):
                first, final = not makes, len(makes) == 3 * KT - 1
                makes.append(lambda e, w=w, x=x, k=k, first=first, final=final: e.matmul(
                    out, w, x[:, k, :], start=first, stop=final))
        m = self.pe.run(makes, *ready, *self.bank_free[bank], *after)
        self.used_by(m)
        return m

    def rows_step(self, name, banks, xh, xl, first, final, *after):
        hi, lo, ready = self.piece(name)
        makes = []
        for tb in range(TB):
            sh, sl = xh[:, tb * P:(tb + 1) * P], xl[:, tb * P:(tb + 1) * P]
            for s, w, st, en in ((sh, hi, first, False), (sh, lo, False, False), (sl, hi, False, final)):
                for half in range(2):
                    b = self.banks[banks[tb * 2 + half]]
                    makes.append(lambda e, b=b, s=s, w=w, half=half, st=st, en=en: e.matmul(
                        b[:, :], s, w[:, half * HALF:(half + 1) * HALF], start=st, stop=en))
        free = [m for b in banks for m in self.bank_free[b]] if first else []
        m = self.pe.run(makes, *ready, *free, *after)
        self.used_by(m)
        return m

    def product_rows(self, name, banks, xh, xl, *after):
        for k in range(KT):
            m = self.rows_step(name, banks, xh[:, k, :], xl[:, k, :], k == 0, k == KT - 1, *(after if k == 0 else ()))
        return m

    def transpose_split(self, src, src_mark, hi, lo, scale=None, tmp=None, dst_free=(), banks=(0, 1, 2, 3)):
        marks = []
        for n in range(KT // 2):
            b = banks[n % len(banks)]
            bank = self.banks[b]
            makes = []
            for i in range(2):
                for tb in range(TB):
                    k = 2 * n + i
                    makes.append(lambda e, i=i, tb=tb, k=k, bank=bank: e.transpose(
                        bank[:, i * SEQ + tb * P:i * SEQ + (tb + 1) * P], src[:, tb, k * P:(k + 1) * P], self.ident))
            t = self.pe.run(makes, src_mark, *self.bank_free[b])
            if hi is not None:
                h, l = hi[:, 2 * n:2 * n + 2, :], lo[:, 2 * n:2 * n + 2, :]
            wide = bank[:, :].rearrange("p (a t) -> p a t", a=2)
            if scale is None:
                a = self.act.do(lambda e: e.activation(h, wide, ACT.Copy), t, *dst_free, chain=False)
                d = self.dve.do(lambda e: e.tensor_tensor(l, wide, h.bitcast(F32), ALU.subtract), t, a, *dst_free,
                                chain=False)
            else:
                for i in range(2):
                    sc = scale(2 * n + i)
                    d = self.dve.do(lambda e: e.tensor_scalar(
                        tmp[:, 2 * n + i, :], bank[:, i * SEQ:(i + 1) * SEQ], sc, None, ALU.mult), t, chain=False)
                if hi is None:
                    self.bank_free[b] = (d,)
                    marks.append(d)
                    continue
                w = tmp[:, 2 * n:2 * n + 2, :]
                a = self.act.do(lambda e: e.activation(h, w, ACT.Copy), d, *dst_free, chain=False)
                d = self.dve.do(lambda e: e.tensor_tensor(l, w, h.bitcast(F32), ALU.subtract), a, *dst_free,
                                chain=False)
            self.bank_free[b] = (a, d)
            marks += [a, d]
        return marks

    def transpose_plain(self, src, src_mark, dst, *after, banks=(4, 5, 6, 7)):
        for n in range(KT // 2):
            b = banks[n % len(banks)]
            bank = self.banks[b]
            makes = []
            for i in range(2):
                for tb in range(TB):
                    k = 2 * n + i
                    makes.append(lambda e, i=i, tb=tb, k=k, bank=bank: e.transpose(
                        bank[:, i * SEQ + tb * P:i * SEQ + (tb + 1) * P], src[:, tb, k * P:(k + 1) * P], self.ident))
            t = self.pe.run(makes, src_mark, *self.bank_free[b])
            m = self.act.do(lambda e: e.activation(dst[:, 2 * n:2 * n + 2, :], bank[:, :].rearrange(
                "p (a t) -> p a t", a=2), ACT.Copy), t, *after, chain=False)
            self.bank_free[b] = (m,)
        return m

    def refresh_xt(self, mark):
        return self.transpose_split(self.resid, mark, self.xt_hi, self.xt_lo, dst_free=(self.pe.last(),))

    def inv_sqrt(self, v, *after):
        a = self.act.do(lambda e: e.activation(v, v, ACT.Sqrt), *after)
        return self.dve.do(lambda e: e.reciprocal(v, v), a)

    def layer_norm(self, ctx, y, y_mark, g, b, *row_marks):
        st = self.sb(ctx, f"ln_stats{self.n_load}", [P, TB, 2, 6], F32)
        mv = self.sb(ctx, f"ln_mv{self.n_load}", [P, TB, 2], F32)
        self.dve.wait(y_mark)
        for tb in range(TB):
            for h in range(2):
                m = self.dve.do(lambda e: e.bn_stats(st[:, tb, h, :], y[:, tb, h * HALF:(h + 1) * HALF]))
        for tb in range(TB):
            m = self.dve.do(lambda e: e.bn_aggr(mv[:, tb, :], st[:, tb, :, :].rearrange("p a b -> p (a b)")))
        rstd = mv[:, :, 1]
        m = self.dve.do(lambda e: e.tensor_scalar(rstd, rstd, LN_EPS, None, ALU.add))
        m = self.inv_sqrt(rstd, m)
        for tb in range(TB):
            self.dve.do(lambda e: e.tensor_scalar(y[:, tb, :], y[:, tb, :], mv[:, tb, 0:1], mv[:, tb, 1:2],
                                                  ALU.subtract, ALU.mult))
        for tb in range(TB):
            self.dve.do(lambda e: e.tensor_tensor(y[:, tb, :], y[:, tb, :], g[:, :], ALU.mult), *row_marks)
        for tb in range(TB):
            m = self.dve.do(lambda e: e.tensor_tensor(self.resid[:, tb, :], y[:, tb, :], b[:, :], ALU.add))
        return m

    def rms_stats(self, src, ss, junk, *after):
        for tb in range(TB):
            m = self.act.do(lambda e: e.activation(junk[:, :], src[:, tb, :], ACT.Square,
                                                   accum_out=ss[:, tb:tb + 1]), *after)
        m = self.dve.do(lambda e: e.tensor_scalar(ss[:, :], ss[:, :], 1.0 / D, RMS_EPS_2, ALU.mult, ALU.add), m)
        return self.inv_sqrt(ss[:, :], m)

    def pre_norm(self, ctx, scale, hi, lo, tmp, dst_free=()):
        xn = self.sb(ctx, f"xn{self.n_load}", [P, TB, D], F32)
        ss = self.sb(ctx, f"ss{self.n_load}", [P, TB], F32)
        m = self.rms_stats(self.resid, ss, xn[:, 0, :])
        for tb in range(TB):
            m = self.dve.do(lambda e: e.tensor_scalar(xn[:, tb, :], self.resid[:, tb, :], ss[:, tb:tb + 1], None,
                                                      ALU.mult), m)
        return self.transpose_split(xn, m, hi, lo, scale=scale, tmp=tmp, dst_free=dst_free)

    def post_norm(self, ctx, y, y_mark, row_name, factor):
        g = self.sb(ctx, f"g{self.n_load}", [P, D], F32)
        junk = self.sb(ctx, f"junk{self.n_load}", [P, D], F32)
        ss = self.sb(ctx, f"pss{self.n_load}", [P, TB], F32)
        gm = self.row(row_name, g[:, :])
        m = self.rms_stats(y, ss, junk, y_mark)
        if factor != 1.0:
            m = self.dve.do(lambda e: e.tensor_scalar(ss[:, :], ss[:, :], factor, None, ALU.mult), m)
        for tb in range(TB):
            self.dve.do(lambda e: e.scalar_tensor_tensor(y[:, tb, :], y[:, tb, :], ss[:, tb:tb + 1], g[:, :],
                                                         ALU.mult, ALU.mult), m, gm)
            m = self.dve.do(lambda e: e.tensor_tensor(self.resid[:, tb, :], self.resid[:, tb, :], y[:, tb, :],
                                                      ALU.add))
        return m

    def close_first(self, ctx, y, tag, banks, m):
        g = self.sb(ctx, f"row_g{tag}", [P, D], F32)
        b = self.sb(ctx, f"row_b{tag}", [P, D], F32)
        gm, bm = self.row(f"ln_g{tag}", g[:, :]), self.row(f"ln_b{tag}", b[:, :])
        for tb in range(TB):
            for h in range(2):
                bk = self.banks[banks[tb * 2 + h]]
                m = self.dve.do(lambda e: e.scalar_tensor_tensor(
                    y[:, tb, h * HALF:(h + 1) * HALF], self.resid[:, tb, h * HALF:(h + 1) * HALF], ALPHA,
                    bk[:, :], ALU.mult, ALU.add), m)
                self.bank_free[banks[tb * 2 + h]] = (m,)
        m = self.layer_norm(ctx, y, m, g, b, gm, bm)
        return self.refresh_xt(m)

    def out_rows(self, banks, dst, m, add=None):
        marks = []
        for tb in range(TB):
            for h in range(2):
                bk, d = self.banks[banks[tb * 2 + h]], dst[:, tb, h * HALF:(h + 1) * HALF]
                if add is None:
                    a = self.act.do(lambda e: e.activation(d, bk[:, :], ACT.Copy), m, chain=False)
                else:
                    a = self.dve.do(lambda e: e.tensor_tensor(d, bk[:, :], add[:, h * HALF:(h + 1) * HALF],
                                                              ALU.add), m)
                self.bank_free[banks[tb * 2 + h]] = (a,)
        return a

    def start(self):
        x = self.dram["x"].rearrange("(b p) d -> p b d", p=P)
        marks = [self.load(self.resid[:, :, :], x), self.load(self.fixed[:, :], self.dram["fixed"]),
                 self.load(self.chan[:, :], self.dram["chan"])]
        for line in (self.pe, self.act, self.dve, self.pool):
            line.wait(*marks)
        if self.stages[0] in ("diff", "peer0", "stick", "peer1"):
            self.refresh_xt(None)

    def finish(self):
        for tb in range(TB):
            self.pool.wait(self.dve.last())
        m = self.load(self.out.rearrange("(b p) d -> p b d", p=P), self.resid[:, :, :])
        self.pool.wait(m)

    def diff(self):
        with ExitStack() as ctx:
            sb = lambda name, shape, dt=F32: self.sb(ctx, "df_" + name, shape, dt)
            c, cm = self.const(ctx, "cos", "sin", "diff_mask")
            small = sb("small", [P, N_SM])
            sm = self.load(small[:, :], self.dram["small"].broadcast_to([P, N_SM]))
            q, k, v = sb("q", [P, TB, D]), sb("k", [P, TB, D]), sb("v", [P, TB, D])
            rot = sb("rot", [P, D])
            qt, kt = sb("qt", [P, KT, SEQ]), sb("kt", [P, KT, SEQ])
            o = sb("o", [P, TB, D])
            ot_hi, ot_lo = sb("ot_hi", [P, KT, SEQ], R32), sb("ot_lo", [P, KT, SEQ], R32)
            neg_lam = sb("neg_lam", [P, 4])
            lp = small[:, 0:256].rearrange("p (a b d) -> p a b d", a=2, b=2)
            lprod = sb("lprod", [P, 2, HD])
            self.dve.do(lambda e: e.tensor_tensor(lprod[:, :, :], lp[:, :, 0, :], lp[:, :, 1, :], ALU.mult), sm, *cm)
            m = self.dve.do(lambda e: e.tensor_reduce(neg_lam[:, 0:2], lprod[:, :, :], AX, ALU.add))
            m = self.act.do(lambda e: e.activation(neg_lam[:, 0:2], neg_lam[:, 0:2], ACT.Exp), m)
            lam_mark = self.dve.do(lambda e: e.scalar_tensor_tensor(
                neg_lam[:, 2:3], neg_lam[:, 1:2], LAMBDA_INIT, neg_lam[:, 0:1], ALU.subtract, ALU.subtract), m)

            marks = []
            for dst, banks in ((q, (0, 1, 2, 3)), (k, (4, 5, 6, 7)), (v, (0, 1, 2, 3))):
                m = self.product_rows("qkv", banks, self.xt_hi, self.xt_lo, self.act.last(), self.dve.last())
                marks.append(self.out_rows(banks, dst, m))
            for dst, mark, t in ((q, marks[0], qt), (k, marks[1], kt)):
                for tb in range(TB):
                    h4 = dst[:, tb, :].rearrange("p (h s d) -> p h s d", s=2, d=HD // 2)
                    r4 = rot[:, :].rearrange("p (h s d) -> p h s d", s=2, d=HD // 2)
                    for s in range(2):
                        sn = bcast(c["sin"][:, tb * HD + s * 32:tb * HD + s * 32 + 32], 1, HEADS)
                        self.dve.do(lambda e: e.tensor_tensor(r4[:, :, s, :], h4[:, :, 1 - s, :], sn, ALU.mult), mark)
                    h3 = dst[:, tb, :].rearrange("p (h d) -> p h d", d=HD)
                    cs = bcast(c["cos"][:, tb * HD:(tb + 1) * HD], 1, HEADS)
                    self.dve.do(lambda e: e.tensor_tensor(h3, h3, cs, ALU.mult))
                    m = self.dve.do(lambda e: e.tensor_tensor(dst[:, tb, :], dst[:, tb, :], rot[:, :], ALU.add))
                self.transpose_plain(dst, m, t)
            self.join()

            scale = HD ** -0.5
            s_ring = Ring([sb(f"s{i}", [P, 2, SEQ]) for i in range(3)])
            a_ring = Ring([sb(f"a{i}", [P, SEQ]) for i in range(3)])
            at_ring = Ring([sb(f"at{i}", [P, SEQ]) for i in range(3)])
            st_ring = Ring([sb(f"st{i}", [P, 8]) for i in range(3)])
            score_bank, turn_bank, out_bank = Ring([0, 1, 2, 3]), Ring([4, 5]), Ring([6, 7])
            for b in range(8):
                self.bank_free[b] = ()
            for tb in range(TB):
                n = (tb + 1) * P
                mask = c["diff_mask"][:, tb * SEQ:tb * SEQ + n]
                for h in range(DIFF_HEADS):
                    s, s_free, s_at = s_ring.take()
                    st, st_free, st_at = st_ring.take()
                    for mp in range(2):
                        bk, b_free, b_at = score_bank.take()
                        bank = self.banks[bk]
                        r = slice(mp * HD, (mp + 1) * HD)
                        pm = self.pe.run([lambda e: e.matmul(bank[:, 0:n], qt[r, h, tb * P:(tb + 1) * P],
                                                             kt[r, h, 0:n], start=True, stop=True)], *b_free)
                        d = self.dve.do(lambda e: e.scalar_tensor_tensor(
                            s[:, mp, 0:n], bank[:, 0:n], scale, mask, ALU.mult, ALU.add), pm, *s_free, *st_free,
                            chain=False)
                        score_bank.give(b_at, d)
                    d = self.dve.do(lambda e: e.tensor_reduce(st[:, 0:2], s[:, :, 0:n], AX, ALU.max, negate=True), d)
                    for mp in range(2):
                        a = self.act.do(lambda e: e.activation(s[:, mp, 0:n], s[:, mp, 0:n], ACT.Exp,
                                                               bias=st[:, mp:mp + 1], accum_out=st[:, 2 + mp:3 + mp]),
                                        d, chain=False)
                    av, a_free, a_at = a_ring.take()
                    self.dve.do(lambda e: e.reciprocal(st[:, 4:6], st[:, 2:4]), a)
                    self.dve.do(lambda e: e.tensor_scalar(st[:, 6:7], st[:, 5:6], neg_lam[:, 2:3], None, ALU.mult),
                                lam_mark)
                    self.dve.do(lambda e: e.tensor_scalar(av[:, 0:n], s[:, 0, 0:n], st[:, 4:5], None, ALU.mult),
                                *a_free)
                    d = self.dve.do(lambda e: e.scalar_tensor_tensor(av[:, 0:n], s[:, 1, 0:n], st[:, 6:7],
                                                                     av[:, 0:n], ALU.mult, ALU.add))
                    s_ring.give(s_at, d)
                    st_ring.give(st_at, d)
                    self.values(av, d, n, tb, h, a_ring, a_at, at_ring, turn_bank, out_bank,
                                v[:, :, h * P:(h + 1) * P], o)
            self.join()
            ss = sb("ss", [P, TB * DIFF_HEADS])
            ov = o[:, :, :].rearrange("p b (h d) -> p (b h) d", d=P)
            sq = q[:, :, :].rearrange("p b (h d) -> p (b h) d", d=P)
            self.dve.do(lambda e: e.tensor_tensor(sq, ov, ov, ALU.mult))
            self.dve.do(lambda e: e.tensor_reduce(ss[:, :], sq, AX, ALU.add))
            m = self.dve.do(lambda e: e.tensor_scalar(ss[:, :], ss[:, :], 1.0 / P, RMS_EPS, ALU.mult, ALU.add))
            m = self.inv_sqrt(ss[:, :], m)
            self.dve.do(lambda e: e.tensor_scalar(ss[:, :], ss[:, :], 1.0 - LAMBDA_INIT, None, ALU.mult))
            self.dve.do(lambda e: e.tensor_tensor(ov, ov, bcast(ss[:, :], 2, P), ALU.mult))
            m = self.dve.do(lambda e: e.tensor_tensor(ov, ov, bcast(small[:, 256:384], 1, TB * DIFF_HEADS), ALU.mult))
            marks = self.transpose_split(o, m, ot_hi, ot_lo)
            m = self.product_rows("w_o_a", (4, 5, 6, 7), ot_hi, ot_lo, *marks)
            self.close_first(ctx, k, "00", (4, 5, 6, 7), m)
            self.join()

    def values(self, av, av_mark, n, tb, h, a_ring, a_at, at_ring, turn_bank, out_bank, v, o):
        at, at_free, at_at = at_ring.take()
        tk, t_free, t_at = turn_bank.take()
        tbank = self.banks[tk]
        t = self.pe.run([lambda e, i=i: e.transpose(tbank[:, i * P:(i + 1) * P], av[:, i * P:(i + 1) * P], self.ident)
                         for i in range(n // P)], av_mark, *t_free)
        a_ring.give(a_at, t)
        a = self.act.do(lambda e: e.activation(at[:, 0:n], tbank[:, 0:n], ACT.Copy), t, *at_free, chain=False)
        turn_bank.give(t_at, a)
        ok, o_free, o_at = out_bank.take()
        obank = self.banks[ok]
        w = v.shape[-1]
        m = self.pe.run([lambda e, i=i: e.matmul(obank[:, 0:w], at[:, i * P:(i + 1) * P], v[:, i, :],
                                                 start=i == 0, stop=i == n // P - 1) for i in range(n // P)],
                        a, *o_free)
        at_ring.give(at_at, m)
        a = self.act.do(lambda e: e.activation(o[:, tb, h * w:(h + 1) * w], obank[:, 0:w], ACT.Copy), m, chain=False)
        out_bank.give(o_at, a)

    def top16(self, lists, vals, idx, n_lists):
        dve = self.dve
        for half in range(2):
            lo, hi = half * 8, half * 8 + 8
            first, found = [], []
            for i in range(n_lists):
                first.append(dve.do(lambda e: e.max(vals[:, i, lo:hi], lists[:, i, :]), chain=(half == 0 and i == 0)
                                    or (half == 1 and i == 0)))
            for i in range(n_lists):
                found.append(dve.do(lambda e: e.max_index(idx[:, i, lo:hi], vals[:, i, lo:hi], lists[:, i, :]),
                                    first[i], chain=False))
            if half == 0:
                for i in range(n_lists):
                    dve.do(lambda e: e.match_replace(lists[:, i, :], vals[:, i, lo:hi], lists[:, i, :], FLT_MIN),
                           found[i], chain=False)
        return dve.last()

    def peer(self, layer):
        tag = f"{layer}1"
        with ExitStack() as slots_ctx:
            slot = self.sb(slots_ctx, f"pr_slot{layer}", [P, 3, SEQ], F32)
            with ExitStack() as ctx:
                sb = lambda name, shape, dt=F32: self.sb(ctx, f"pr{layer}_" + name, shape, dt)
                qt = sb("qt", [P, PH, SEQ])
                keys = sb("keys", [P, PH, 2 * NKEY])
                km = self.load(keys[:, :, :], self.dram["keys"][layer])
                marks = []
                for h in range(PH):
                    b = h % 4
                    m = self.product_cols("pq", b, self.xt_hi, self.xt_lo, self.act.last(), self.dve.last())
                    a = self.act.do(lambda e: e.activation(qt[:, h, :], self.banks[b][:, 0:SEQ], ACT.Copy), m,
                                    chain=False)
                    self.bank_free[b] = (a,)
                    marks.append(a)
                sc = [sb(f"scores{tb}", [P, 2 * PH, NKEY]) for tb in range(TB)]
                cand = sb("cand", [P, PH, TOPK * TOPK])
                eq = sb("eq", [P, PH, TOPK * TOPK])
                vals, idx = sb("vals", [P, 2 * PH, TOPK]), sb("idx", [P, 2 * PH, TOPK], U32)
                idxf = sb("idxf", [P, 2 * PH, TOPK])
                gs, gi = sb("gs", [P, PH, TOPK]), sb("gi", [P, PH, TOPK], U32)
                gab, gabf = sb("gab", [P, PH, TOPK], U32), sb("gabf", [P, PH, TOPK])
                sel = sb("sel", [P, 3, PH * TOPK])
                den = sb("den", [P, PH])
                score_bank = Ring([4, 5, 6, 7])
                for tb in range(TB):
                    for h in range(PH):
                        bk, b_free, b_at = score_bank.take()
                        bank = self.banks[bk]
                        m = self.pe.run([lambda e: e.matmul(bank[:, 0:2 * NKEY], qt[:, h, tb * P:(tb + 1) * P],
                                                            keys[:, h, :], start=True, stop=True)],
                                        marks[h], km, *b_free, *self.bank_free[bk])
                        a = self.act.do(lambda e: e.activation(
                            sc[tb][:, 2 * h:2 * h + 2, :], bank[:, 0:2 * NKEY].rearrange("p (c k) -> p c k", c=2),
                            ACT.Copy), m, chain=False)
                        score_bank.give(b_at, a)
                        self.bank_free[bk] = (a,)
                    ready = a
                    self.dve.wait(ready)
                    self.top16(sc[tb], vals, idx, 2 * PH)
                    self.dve.do(lambda e: e.tensor_copy(idxf[:, :, :], idx[:, :, :]))
                    v4 = vals[:, :, :].rearrange("p (h c) k -> p h c k", c=2)
                    i4 = idxf[:, :, :].rearrange("p (h c) k -> p h c k", c=2)
                    c4 = cand[:, :, :].rearrange("p h (a b) -> p h a b", a=TOPK)
                    e4 = eq[:, :, :].rearrange("p h (a b) -> p h a b", a=TOPK)
                    self.dve.do(lambda e: e.tensor_tensor(c4, bcast(v4[:, :, 0, :], 3, TOPK),
                                                          bcast(v4[:, :, 1, :], 2, TOPK), ALU.add))
                    m = self.top16(cand, gs, gi, PH)
                    gate = sel[:, 2, :].rearrange("p (h k) -> p h k", h=PH)
                    m = self.dve.do(lambda e: e.tensor_tensor(gate, gs[:, :, :], bcast(gs[:, :, 0], 2, TOPK),
                                                              ALU.subtract))
                    a = self.act.do(lambda e: e.activation(gate, gate, ACT.Exp), m)
                    self.dve.do(lambda e: e.tensor_reduce(den[:, :], gate, AX, ALU.add), a)
                    self.dve.do(lambda e: e.reciprocal(den[:, :], den[:, :]))
                    self.dve.do(lambda e: e.tensor_tensor(gate, gate, bcast(den[:, :], 2, TOPK), ALU.mult))
                    iota16 = bcast(bcast(self.iota[:, 0:TOPK], 1, TOPK), 1, PH)
                    for half in range(2):
                        op, by = ((ALU.logical_shift_right, 4), (ALU.bitwise_and, 15))[half]
                        self.dve.do(lambda e: e.tensor_scalar(gab[:, :, :], gi[:, :, :], by, None, op))
                        self.dve.do(lambda e: e.tensor_copy(gabf[:, :, :], gab[:, :, :]))
                        self.dve.do(lambda e: e.tensor_tensor(e4, bcast(gabf[:, :, :], 3, TOPK), iota16,
                                                              ALU.is_equal))
                        self.dve.do(lambda e: e.tensor_tensor(e4, e4, bcast(i4[:, :, half, :], 2, TOPK), ALU.mult))
                        m = self.dve.do(lambda e: e.tensor_reduce(
                            sel[:, half, :].rearrange("p (h k) -> p h k", h=PH), e4, AX, ALU.add))
                    bank = self.banks[0]
                    t = self.pe.run([lambda e, i=i: e.transpose(bank[:, i * P:(i + 1) * P], sel[:, i, :], self.ident)
                                     for i in range(3)], m, *self.bank_free[0])
                    a = self.act.do(lambda e: e.activation(
                        slot[:, :, tb * P:(tb + 1) * P], bank[:, 0:3 * P].rearrange("p (i t) -> p i t", i=3),
                        ACT.Copy), t)
                    self.bank_free[0] = (a,)
                    self.dve.wait(t)
                self.join()
            with ExitStack() as gctx:
                gates = self.sb(gctx, f"gates{layer}", [P, NKEY, SEQ], F32)
                with ExitStack() as ctx:
                    N = 4
                    hot_ring = Ring([(self.sb(ctx, f"hot_i{layer}{i}", [P, N, P], F32),
                                      self.sb(ctx, f"hot_j{layer}{i}", [P, N, P], F32)) for i in range(2)])
                    g_bank = Ring([0, 1, 2, 3])
                    for t0 in range(0, SEQ, N):
                        (hi_, hj), h_free, h_at = hot_ring.take()
                        for i in range(N):
                            t = t0 + i
                            self.dve.do(lambda e: e.tensor_scalar(
                                hi_[:, i, :], self.iota, slot[:, 0, t:t + 1], None, ALU.is_equal), *h_free,
                                chain=False)
                            d = self.dve.do(lambda e: e.tensor_scalar(
                                hj[:, i, :], self.iota, slot[:, 1, t:t + 1], slot[:, 2, t:t + 1], ALU.is_equal,
                                ALU.mult), chain=False)
                        bk, b_free, b_at = g_bank.take()
                        bank = self.banks[bk]
                        m = self.pe.run([lambda e, i=i, bank=bank: e.matmul(bank[:, i * P:(i + 1) * P], hj[:, i, :],
                                                                            hi_[:, i, :], start=True, stop=True)
                                         for i in range(N)], d, *b_free)
                        hot_ring.give(h_at, m)
                        a = self.act.do(lambda e: e.activation(
                            gates[:, :, t0:t0 + N].rearrange("p i t -> p t i"),
                            bank[:, :].rearrange("p (t i) -> p t i", t=N), ACT.Copy), m, chain=False)
                        g_bank.give(b_at, a)
                    self.join()
                with ExitStack() as ctx:
                    g_ring = Ring([self.sb(ctx, f"act{layer}{i}", [P, SEQ], F32) for i in range(2)])
                    gh_ring = Ring([(self.sb(ctx, f"act_hi{layer}{i}", [P, SEQ], R32),
                                     self.sb(ctx, f"act_lo{layer}{i}", [P, SEQ], R32)) for i in range(2)])
                    def activate(i, bank, m):
                        g, g_free, g_at = g_ring.take()
                        a = self.act.do(lambda e: e.activation(g[:, :], bank[:, 0:SEQ], ACT.Gelu), m, *g_free,
                                        chain=False)
                        d = self.dve.do(lambda e: e.tensor_tensor(g[:, :], g[:, :], gates[:, i, :], ALU.mult), a,
                                        chain=False)
                        return (g, g_ring, g_at), d, a
                    m = self.dense_pair("u", "v", NKEY, 1, activate, gh_ring)
                    self.join()
            with ExitStack() as ctx:
                y = self.sb(ctx, f"pr_y{layer}", [P, TB, D], F32)
                self.close_first(ctx, y, tag, (4, 5, 6, 7), m)
                self.join()

    def dense_pair(self, up, down, tiles, n_up, activate, gh_ring, xh=None, xl=None, after=()):
        xh, xl = xh or self.xt_hi, xl or self.xt_lo
        for b in range(4):
            self.bank_free[b] = ()
        hidden = {}
        turn = 0

        def hid(i):
            nonlocal turn
            banks = []
            for _ in range(n_up):
                b = turn % 4
                turn += 1
                m = self.product_cols(up, b, xh, xl, *(after if i == 0 else ()))
                banks.append(b)
            bk = [self.banks[b] for b in banks]
            (g, ring, at), d, freed = activate(i, bk[0] if n_up == 1 else bk, m)
            for b in banks:
                self.bank_free[b] = (freed,)
            (gh, gl), gh_free, gh_at = gh_ring.take()
            a = self.act.do(lambda e: e.activation(gh[:, :], g[:, :], ACT.Copy), d, *gh_free, chain=False)
            d = self.dve.do(lambda e: e.tensor_tensor(gl[:, :], g[:, :], gh[:, :].bitcast(F32), ALU.subtract), a,
                            *gh_free, chain=False)
            ring.give(at, d)
            hidden[i] = (gh, gl, gh_at, a, d)

        hid(0)
        for i in range(tiles):
            if i + 1 < tiles:
                hid(i + 1)
            gh, gl, gh_at, a, d = hidden.pop(i)
            m = self.rows_step(down, (4, 5, 6, 7), gh[:, :], gl[:, :], i == 0, i == tiles - 1, a, d)
            gh_ring.give(gh_at, m)
        return m

    def stick(self):
        with ExitStack() as ctx:
            sb = lambda name, shape, dt=F32: self.sb(ctx, "sk_" + name, shape, dt)
            c, cm = self.const(ctx, "sb_keep", "sb_drop")
            self.dve.wait(*cm)
            kt, qt = sb("kt", [P, KT, SEQ]), sb("qt", [P, KT, SEQ])
            v, y, o = sb("v", [P, TB, D]), sb("y", [P, TB, D]), sb("o", [P, TB, D])
            ot_hi, ot_lo = sb("ot_hi", [P, KT, SEQ], R32), sb("ot_lo", [P, KT, SEQ], R32)
            last = (self.act.last(), self.dve.last())
            for j in range(KT):
                b = j % 4
                m = self.product_cols("kv_k", b, self.xt_hi, self.xt_lo, *last)
                a = self.act.do(lambda e: e.activation(kt[:, j, :], self.banks[b][:, 0:SEQ], ACT.Copy), m, chain=False)
                self.bank_free[b] = (a,)
            m = self.product_rows("kv_v", (4, 5, 6, 7), self.xt_hi, self.xt_lo)
            self.out_rows((4, 5, 6, 7), v, m)
            for j in range(KT):
                b = j % 4
                m = self.product_cols("sb_q", b, self.xt_hi, self.xt_lo)
                a = self.act.do(lambda e: e.activation(qt[:, j, :], self.banks[b][:, 0:SEQ], ACT.Copy), m, chain=False)
                self.bank_free[b] = (a,)
            self.join()
            scale = HD ** -0.5
            l_ring = Ring([sb(f"l{i}", [P, SEQ]) for i in range(3)])
            c_ring = Ring([sb(f"c{i}", [P, SEQ]) for i in range(3)])
            a_ring = Ring([sb(f"a{i}", [P, SEQ]) for i in range(3)])
            at_ring = Ring([sb(f"at{i}", [P, SEQ]) for i in range(3)])
            ones = sb("ones", [P, SEQ])
            self.dve.do(lambda e: e.memset(ones[:, :], 1.0))
            score_bank, turn_bank, out_bank = Ring([0, 1, 2, 3]), Ring([4, 5]), Ring([6, 7])
            for tb in range(TB):
                n = (tb + 1) * P
                keep, drop = (c[x][:, tb * SEQ:tb * SEQ + n] for x in ("sb_keep", "sb_drop"))
                for h in range(HEADS):
                    r = slice((h % 2) * HD, (h % 2 + 1) * HD)
                    bk, b_free, b_at = score_bank.take()
                    z = self.banks[bk]
                    pm = self.pe.run([lambda e: e.matmul(z[:, 0:n], qt[r, h // 2, tb * P:(tb + 1) * P],
                                                         kt[r, h // 2, 0:n], start=True, stop=True)], *b_free)
                    l, l_free, l_at = l_ring.take()
                    cu, c_free, c_at = c_ring.take()
                    self.act.do(lambda e: e.activation(l[:, 0:n], z[:, 0:n], ACT.Abs, scale=scale), pm, *l_free)
                    self.act.do(lambda e: e.activation(l[:, 0:n], l[:, 0:n], ACT.Exp, scale=-1.0))
                    a = self.act.do(lambda e: e.activation(l[:, 0:n], l[:, 0:n], ACT.Ln, bias=1.0))
                    self.dve.do(lambda e: e.tensor_scalar(cu[:, 0:n], z[:, 0:n], scale, 0.0, ALU.mult, ALU.max),
                                a, *c_free)
                    self.dve.do(lambda e: e.tensor_tensor(l[:, 0:n], l[:, 0:n], cu[:, 0:n], ALU.add))
                    self.dve.do(lambda e: e.tensor_tensor(l[:, 0:n], l[:, 0:n], keep, ALU.mult))
                    self.dve.do(lambda e: e.tensor_tensor_scan(cu[:, 0:n][:, ::-1], ones[:, 0:n], l[:, 0:n][:, ::-1],
                                                               0.0, ALU.mult, ALU.add))
                    self.dve.do(lambda e: e.tensor_tensor(cu[:, 0:n], cu[:, 0:n], drop, ALU.add))
                    d = self.dve.do(lambda e: e.scalar_tensor_tensor(cu[:, 0:n], z[:, 0:n], scale, cu[:, 0:n],
                                                                     ALU.mult, ALU.subtract))
                    l_ring.give(l_at, d)
                    score_bank.give(b_at, d)
                    av, a_free, a_at = a_ring.take()
                    a = self.act.do(lambda e: e.activation(av[:, 0:n], cu[:, 0:n], ACT.Exp), d, *a_free)
                    c_ring.give(c_at, a)
                    self.values(av, a, n, tb, h, a_ring, a_at, at_ring, turn_bank, out_bank,
                                v[:, :, h * HD:(h + 1) * HD], o)
            self.join()
            marks = self.transpose_split(o, self.act.last(), ot_hi, ot_lo)
            m = self.product_rows("w_o_b", (4, 5, 6, 7), ot_hi, ot_lo, *marks)
            self.close_first(ctx, y, "10", (4, 5, 6, 7), m)
            self.join()

    def ffn(self, layer, which):
        tag = f"{layer}{which}"
        with ExitStack() as ctx:
            tmp = self.sb(ctx, f"ff_tmp{tag}", [P, KT, SEQ], F32)
            marks = self.pre_norm(ctx, lambda j: self.ch("pre", (layer * 3 + 2 * which) * 8 + j), self.xt_hi,
                                  self.xt_lo, tmp, (self.pe.last(),))
            g_ring = Ring([self.sb(ctx, f"ff_g{tag}{i}", [P, SEQ], F32) for i in range(2)])
            gh_ring = Ring([(self.sb(ctx, f"ff_hi{tag}{i}", [P, SEQ], R32),
                             self.sb(ctx, f"ff_lo{tag}{i}", [P, SEQ], R32)) for i in range(2)])

            def activate(i, banks, m):
                g, g_free, g_at = g_ring.take()
                a = self.act.do(lambda e: e.activation(g[:, :], banks[0][:, 0:SEQ], ACT.Silu), m, *g_free,
                                chain=False)
                d = self.dve.do(lambda e: e.tensor_tensor(g[:, :], banks[1][:, 0:SEQ], g[:, :], ALU.mult), a, m,
                                chain=False)
                return (g, g_ring, g_at), d, d
            m = self.dense_pair("up", "down", FT, 2, activate, gh_ring, after=marks)
            y = self.sb(ctx, f"ff_y{tag}", [P, TB, D], F32)
            m = self.out_rows((4, 5, 6, 7), y, m)
            self.post_norm(ctx, y, m, f"post{layer}{(1, 5)[which]}", 0.5)
            self.join()

    def swa_kv(self):
        ctx = self.ctx
        self.k_sh = self.sb(ctx, "k_shared", [P, KV_HEADS, SEQ], F32)
        self.v_sh = self.sb(ctx, "v_shared", [P, TB, 256], F32)
        with ExitStack() as ctx:
            tmp = self.sb(ctx, "kv_tmp", [P, KT, SEQ], F32)
            bv = self.sb(ctx, "kv_bv", [P, 256], F32)
            o = SM["b_v"][0]
            bm = self.load(bv[:, :], self.dram["small"][:, o:o + 256].broadcast_to([P, 256]))
            marks = self.pre_norm(ctx, lambda j: self.ch("kv_g", j), self.xt_hi, self.xt_lo, tmp, (self.pe.last(),))
            for g in range(KV_HEADS):
                m = self.product_cols("kv2_k", g, self.xt_hi, self.xt_lo, *marks)
                a = self.dve.do(lambda e: e.tensor_scalar(self.k_sh[:, g, :], self.banks[g][:, 0:SEQ],
                                                          self.ch("b_k", g), None, ALU.add), m)
                self.bank_free[g] = (a,)
            for p in range(2):
                hi, lo, ready = self.piece("kv2_v")
                makes = []
                for tb in range(TB):
                    out = self.banks[4 + tb][:, 0:256]
                    for k in range(4):
                        kk = p * 4 + k
                        xh, xl = (x[:, kk, tb * P:(tb + 1) * P] for x in (self.xt_hi, self.xt_lo))
                        wh, wl = (w[:, k * 256:(k + 1) * 256] for w in (hi, lo))
                        for s, w, st, en in ((xh, wh, kk == 0, False), (xh, wl, False, False),
                                             (xl, wh, False, kk == KT - 1)):
                            makes.append(lambda e, out=out, s=s, w=w, st=st, en=en: e.matmul(
                                out, s, w, start=st, stop=en))
                m = self.pe.run(makes, *ready, *self.bank_free[4], *self.bank_free[5])
                self.used_by(m)
            for tb in range(TB):
                a = self.dve.do(lambda e: e.tensor_tensor(self.v_sh[:, tb, :], self.banks[4 + tb][:, 0:256],
                                                          bv[:, :], ALU.add), m, bm)
                self.bank_free[4 + tb] = (a,)
            self.join()

    def swa(self):
        with ExitStack() as ctx:
            sb = lambda name, shape, dt=F32: self.sb(ctx, "sw_" + name, shape, dt)
            c, cm = self.const(ctx, "swa_mask")
            sinks, bo = sb("sinks", [P, HEADS]), sb("bo", [P, D])
            o_ = SM["sinks"][0]
            cm += [self.load(sinks[:, :], self.dram["small"][:, o_:o_ + HEADS].broadcast_to([P, HEADS])),
                   self.row("b_o", bo[:, :])]
            tmp, qt = sb("tmp", [P, KT, SEQ]), sb("qt", [P, KT, SEQ])
            o, y = sb("o", [P, TB, D]), sb("y", [P, TB, D])
            ot_hi, ot_lo = sb("ot_hi", [P, KT, SEQ], R32), sb("ot_lo", [P, KT, SEQ], R32)
            marks = self.pre_norm(ctx, lambda j: self.ch("pre", 4 * 8 + j), self.xt_hi, self.xt_lo, tmp,
                                  (self.pe.last(),))
            for j in range(KT):
                b = j % 4
                m = self.product_cols("sw_q", b, self.xt_hi, self.xt_lo, *marks)
                a = self.dve.do(lambda e: e.tensor_scalar(qt[:, j, :], self.banks[b][:, 0:SEQ], self.ch("b_q", j),
                                                          None, ALU.add), m)
                self.bank_free[b] = (a,)
            self.dve.wait(*cm)
            self.join()
            scale = HD ** -0.5
            s_ring = Ring([sb(f"s{i}", [P, SEQ]) for i in range(3)])
            a_ring = Ring([sb(f"a{i}", [P, SEQ]) for i in range(3)])
            at_ring = Ring([sb(f"at{i}", [P, SEQ]) for i in range(3)])
            st_ring = Ring([sb(f"st{i}", [P, 8]) for i in range(3)])
            score_bank, turn_bank, out_bank = Ring([0, 1, 2, 3]), Ring([4, 5]), Ring([6, 7])
            for tb in range(TB):
                n = (tb + 1) * P
                mask = c["swa_mask"][:, tb * SEQ:tb * SEQ + n]
                for h in range(HEADS):
                    r = slice((h % 2) * HD, (h % 2 + 1) * HD)
                    g = h // GROUP
                    bk, b_free, b_at = score_bank.take()
                    bank = self.banks[bk]
                    s, s_free, s_at = s_ring.take()
                    st, st_free, st_at = st_ring.take()
                    pm = self.pe.run([lambda e: e.matmul(bank[:, 0:n], qt[r, h // 2, tb * P:(tb + 1) * P],
                                                         self.k_sh[r, g, 0:n], start=True, stop=True)], *b_free)
                    d = self.dve.do(lambda e: e.scalar_tensor_tensor(
                        s[:, 0:n], bank[:, 0:n], scale, mask, ALU.mult, ALU.add), pm, *s_free, *st_free)
                    score_bank.give(b_at, d)
                    self.dve.do(lambda e: e.tensor_reduce(st[:, 0:1], s[:, 0:n], AX, ALU.max))
                    d = self.dve.do(lambda e: e.tensor_scalar(st[:, 1:2], st[:, 0:1], sinks[:, h:h + 1], -1.0,
                                                              ALU.max, ALU.mult))
                    a = self.act.do(lambda e: e.activation(s[:, 0:n], s[:, 0:n], ACT.Exp, bias=st[:, 1:2],
                                                           accum_out=st[:, 2:3]), d, chain=False)
                    a = self.act.do(lambda e: e.activation(st[:, 3:4], sinks[:, h:h + 1], ACT.Exp, bias=st[:, 1:2]),
                                    chain=False)
                    self.dve.do(lambda e: e.tensor_tensor(st[:, 4:5], st[:, 2:3], st[:, 3:4], ALU.add), a)
                    self.dve.do(lambda e: e.reciprocal(st[:, 5:6], st[:, 4:5]))
                    av, a_free, a_at = a_ring.take()
                    d = self.dve.do(lambda e: e.tensor_scalar(av[:, 0:n], s[:, 0:n], st[:, 5:6], None, ALU.mult),
                                    *a_free)
                    s_ring.give(s_at, d)
                    st_ring.give(st_at, d)
                    self.values(av, d, n, tb, h, a_ring, a_at, at_ring, turn_bank, out_bank,
                                self.v_sh[:, :, g * HD:(g + 1) * HD], o)
            self.join()
            marks = self.transpose_split(o, self.act.last(), ot_hi, ot_lo)
            m = self.product_rows("sw_o", (4, 5, 6, 7), ot_hi, ot_lo, *marks)
            m = self.out_rows((4, 5, 6, 7), y, m, add=bo)
            self.post_norm(ctx, y, m, "post13", 1.0)
            self.join()

    def mix(self, i, u, xx, xm, *after):
        for j in range(KT):
            m = self.dve.do(lambda e: e.scalar_tensor_tensor(xm[:, j, :], xx[:, j, :], self.ch("mu", i * 8 + j),
                                                             u[:, j, :], ALU.mult, ALU.add), *after, chain=False)
        return m

    def mix_split(self, i, u, xx, xm, *after):
        m = self.mix(i, u, xx, xm, *after)
        free = self.pe.last()
        a = self.act.do(lambda e: e.activation(self.xt_hi[:, :, :], xm[:, :, :], ACT.Copy), m, free)
        return self.dve.do(lambda e: e.tensor_tensor(self.xt_lo[:, :, :], xm[:, :, :],
                                                     self.xt_hi[:, :, :].bitcast(F32), ALU.subtract), a, free)

    def rwkv(self):
        dve, act, pe = self.dve, self.act, self.pe
        with ExitStack() as ctx:
            sb = lambda name, shape, dt=F32: self.sb(ctx, "rw_" + name, shape, dt)
            ar = sb("ar", [P, KT, TB, 2, P])
            bt, kt = sb("bt", [P, KT, SEQ]), sb("kt", [P, KT, SEQ])
            v, g = sb("v", [P, TB, D]), sb("g", [P, TB, D])
            bonus, carry = sb("bonus", [P, TB, HEADS]), sb("carry", [P, KT])
            with ExitStack() as c1:
                self.rwkv_inputs(c1, ar, bt, kt, v, g, bonus, carry)
                self.join()
            y = sb("y", [P, TB, D])
            with ExitStack() as c2:
                self.rwkv_chunks(c2, ar, bt, kt, v, y, carry)
                self.join()
            with ExitStack() as c3:
                gn_g, gn_b = self.sb(c3, "gn_g", [P, D]), self.sb(c3, "gn_b", [P, D])
                rm = [self.row("gn_g", gn_g[:, :]), self.row("gn_b", gn_b[:, :])]
                sq = self.sb(c3, "gn_sq", [P, TB, D])
                mean, var = self.sb(c3, "gn_mean", [P, TB * HEADS]), self.sb(c3, "gn_var", [P, TB * HEADS])
                heads = lambda t: t[:, :, :].rearrange("p b (h i) -> p (b h) i", i=HD)
                dve.do(lambda e: e.tensor_reduce(mean[:, :], heads(y), AX, ALU.add))
                dve.do(lambda e: e.tensor_scalar(mean[:, :], mean[:, :], 1.0 / HD, None, ALU.mult))
                dve.do(lambda e: e.tensor_tensor(heads(y), heads(y), bcast(mean[:, :], 2, HD), ALU.subtract))
                dve.do(lambda e: e.tensor_tensor(heads(sq), heads(y), heads(y), ALU.mult))
                dve.do(lambda e: e.tensor_reduce(var[:, :], heads(sq), AX, ALU.add))
                m = dve.do(lambda e: e.tensor_scalar(var[:, :], var[:, :], 1.0 / HD, GN_EPS, ALU.mult, ALU.add))
                self.inv_sqrt(var[:, :], m)
                dve.do(lambda e: e.tensor_tensor(heads(y), heads(y), bcast(var[:, :], 2, HD), ALU.mult))
                dve.wait(*rm)
                dve.do(lambda e: e.tensor_tensor(heads(sq), heads(v),
                                                 bcast(bonus[:, :, :].rearrange("p b h -> p (b h)"), 2, HD), ALU.mult))
                for tb in range(TB):
                    dve.do(lambda e: e.tensor_tensor(y[:, tb, :], y[:, tb, :], gn_g[:, :], ALU.mult))
                    dve.do(lambda e: e.tensor_tensor(y[:, tb, :], y[:, tb, :], gn_b[:, :], ALU.add))
                    dve.do(lambda e: e.tensor_tensor(y[:, tb, :], y[:, tb, :], sq[:, tb, :], ALU.add))
                    m = dve.do(lambda e: e.tensor_tensor(y[:, tb, :], y[:, tb, :], g[:, tb, :], ALU.mult))
                marks = self.transpose_split(y, m, self.xt_hi, self.xt_lo, dst_free=(pe.last(),))
                m = self.product_rows("rw_o", (4, 5, 6, 7), self.xt_hi, self.xt_lo, *marks)
                m = self.out_rows((4, 5, 6, 7), y, m)
                self.post_norm(c3, y, m, "post03", 1.0)
                self.join()

    def rwkv_inputs(self, ctx, ar, bt, kt, v, g, bonus, carry):
        dve, act, pe = self.dve, self.act, self.pe
        sb = lambda name, shape, dt=F32: self.sb(ctx, "ri_" + name, shape, dt)
        c, cm = self.const(ctx, "pair_ones", "head_ones")
        lora = {}
        for name, shape in (("w1", [P, KT, 64]), ("a1", [P, KT, 64]), ("g1", [P, KT, P]), ("w2", [64, D]),
                            ("a2", [64, D]), ("g2", [P, D])):
            lora[name] = sb(name, shape)
            src = self.dram["lora_" + name]
            if name[1] == "1":
                src = src.rearrange("(k p) n -> p k n", p=P)
            full = lora[name][:, :, :] if name[1] == "1" else lora[name][:, :]
            cm.append(self.load(full, src))
        u, xx, r = sb("u", [P, KT, SEQ]), sb("xx", [P, KT, SEQ]), sb("r", [P, KT, SEQ])
        ld = sb("ld", [P, KT, SEQ])
        hid = [sb(f"hid{i}", [P, SEQ]) for i in range(3)]
        with ExitStack() as c0:
            self.pre_norm(c0, lambda j: self.ch("pre", 8 + j), None, None, u)
            self.join()
        dve.do(lambda e: e.tensor_scalar(xx[:, :, 0:1], u[:, :, 0:1], -1.0, None, ALU.mult))
        dve.do(lambda e: e.tensor_tensor(xx[:, :, 1:SEQ], u[:, :, 0:SEQ - 1], u[:, :, 1:SEQ], ALU.subtract))
        with ExitStack() as c0:
            xm = [self.sb(c0, f"ri_xm{i}", [P, KT, SEQ]) for i in range(2)]
            pe.wait(*cm)
            for n, (i, w1, w2, rank, f1) in enumerate(((1, "w1", "w2", 64, ACT.Tanh), (4, "a1", "a2", 64, ACT.Copy),
                                                       (5, "g1", "g2", 128, ACT.Sigmoid))):
                x = xm[n % 2]
                m = self.mix(i, u, xx, x, dve.last(), pe.last())
                b = self.banks[n]
                m = pe.run([lambda e, k=k: e.matmul(b[0:rank, 0:SEQ], lora[w1][:, k, :], x[:, k, :],
                                                    start=k == 0, stop=k == KT - 1) for k in range(KT)],
                           m, *self.bank_free[n])
                a = act.do(lambda e: e.activation(hid[n][0:rank, :], b[0:rank, 0:SEQ], f1), m)
                self.bank_free[n] = (a,)
                if n < 2:
                    dst, bias = ((ld, "w0"), (bt, "a0"))[n]
                    for j in range(KT):
                        bb = 3 + j % 4
                        o = self.banks[bb][:, 0:SEQ]
                        m = pe.run([lambda e: e.matmul(o, lora[w2][0:rank, j * P:(j + 1) * P], hid[n][0:rank, :],
                                                       start=True, stop=True)], a, *self.bank_free[bb])
                        s = act.do(lambda e: e.activation(dst[:, j, :], o, ACT.Sigmoid, bias=self.ch(bias, j)), m,
                                   chain=False)
                        self.bank_free[bb] = (s,)
                else:
                    for tb in range(TB):
                        for h in range(2):
                            bb = 4 + tb * 2 + h
                            m = pe.run([lambda e: e.matmul(self.banks[bb][:, :], hid[n][:, tb * P:(tb + 1) * P],
                                                           lora[w2][:, h * HALF:(h + 1) * HALF], start=True,
                                                           stop=True)], a, *self.bank_free[bb])
                            s = act.do(lambda e: e.activation(g[:, tb, h * HALF:(h + 1) * HALF],
                                                              self.banks[bb][:, :], ACT.Copy), m, chain=False)
                            self.bank_free[bb] = (s,)
            for n, (i, name, dst) in enumerate(((0, "rw_r", r), (2, "rw_k", kt))):
                m = self.mix_split(i, u, xx, xm[n % 2], pe.last(), act.last(), dve.last())
                for j in range(KT):
                    b = j % 4
                    m2 = self.product_cols(name, b, self.xt_hi, self.xt_lo, m, act.last())
                    a = act.do(lambda e: e.activation(dst[:, j, :], self.banks[b][:, 0:SEQ], ACT.Copy), m2,
                               chain=False)
                    self.bank_free[b] = (a,)
            m = self.mix_split(3, u, xx, xm[0], pe.last(), act.last(), dve.last())
            m = self.product_rows("rw_v", (4, 5, 6, 7), self.xt_hi, self.xt_lo, m, act.last())
            self.out_rows((4, 5, 6, 7), v, m)
            self.join()
        with ExitStack() as c0:
            t = self.sb(c0, "ri_t", [P, KT, SEQ])
            kk, cs = self.sb(c0, "ri_kk", [P, KT, SEQ]), u
            dec = xx
            for j in range(KT):
                dve.do(lambda e: e.tensor_scalar(kk[:, j, :], kt[:, j, :], self.ch("k_k", j), None, ALU.mult))
            m = dve.do(lambda e: e.tensor_tensor(t[:, :, :], kk[:, :, :], kk[:, :, :], ALU.mult))
            for j in range(KT):
                b = j % 4
                o = self.banks[b][:, 0:SEQ]
                pm = pe.run([lambda e: e.matmul(o, c["pair_ones"][:, :], t[:, j, :], start=True, stop=True)], m,
                            *self.bank_free[b])
                a = act.do(lambda e: e.activation(dec[:, j, :], o, ACT.Sqrt), pm, chain=False)
                self.bank_free[b] = (a,)
            dve.do(lambda e: e.tensor_scalar(dec[:, :, :], dec[:, :, :], 1e-12, None, ALU.max), a)
            dve.do(lambda e: e.reciprocal(dec[:, :, :], dec[:, :, :]))
            dve.do(lambda e: e.tensor_tensor(kk[:, :, :], kk[:, :, :], dec[:, :, :], ALU.mult), pe.last())
            for j in range(KT):
                dve.do(lambda e: e.tensor_scalar(t[:, j, :], bt[:, j, :], 1.0, self.ch("k_a", j), ALU.subtract,
                                                 ALU.mult))
            dve.do(lambda e: e.scalar_tensor_tensor(kt[:, :, :], t[:, :, :], 1.0, kt[:, :, :], ALU.add, ALU.mult))
            dve.do(lambda e: e.tensor_tensor(bt[:, :, :], bt[:, :, :], kk[:, :, :], ALU.mult))
            for j in range(KT):
                m = dve.do(lambda e: e.scalar_tensor_tensor(t[:, j, :], r[:, j, :], self.ch("r_k", j), kt[:, j, :],
                                                            ALU.mult, ALU.mult))
            for tb in range(TB):
                o = self.banks[4 + tb][:, 0:HEADS]
                pm = pe.run([lambda e, j=j: e.matmul(o, t[:, j, tb * P:(tb + 1) * P],
                                                     c["head_ones"][:, j * HEADS:(j + 1) * HEADS], start=j == 0,
                                                     stop=j == KT - 1) for j in range(KT)],
                            m, *self.bank_free[4 + tb])
                a = act.do(lambda e: e.activation(bonus[:, tb, :], o, ACT.Copy), pm)
                self.bank_free[4 + tb] = (a,)
            dve.do(lambda e: e.tensor_scalar(ld[:, :, :], ld[:, :, :], -math.exp(-0.5), None, ALU.mult))
            dve.do(lambda e: e.memset(t[:, :, :], 1.0), pe.last())
            t4 = t[:, :, :].rearrange("p k (b t) -> p k b t", b=TB)
            dve.do(lambda e: e.memset(t4[:, :, :, 0:1], 0.0))
            flat = lambda a: a[:, :, :].rearrange("p k t -> p (k t)")
            dve.do(lambda e: e.tensor_tensor_scan(flat(cs), flat(t), flat(ld), 0.0, ALU.mult, ALU.add))
            cs4 = cs[:, :, :].rearrange("p k (b t) -> p k b t", b=TB)
            d4 = dec[:, :, :].rearrange("p k (b t) -> p k b t", b=TB)
            ld4 = ld[:, :, :].rearrange("p k (b t) -> p k b t", b=TB)
            mid = cs4[:, :, :, P // 2 - 1]
            dve.do(lambda e: e.tensor_tensor(d4, cs4, bcast(mid, 3, P), ALU.subtract))
            m = dve.do(lambda e: e.tensor_tensor(carry[:, :], d4[:, :, 0, P - 1], mid[:, :, 1], ALU.add))
            m = dve.do(lambda e: e.tensor_tensor(ld[:, :, :], dec[:, :, :], ld[:, :, :], ALU.subtract))
            act.do(lambda e: e.activation(carry[:, :], carry[:, :], ACT.Exp), m)
            a = act.do(lambda e: e.activation(ld[:, :, :], ld[:, :, :], ACT.Exp))
            ar5 = lambda w: ar[:, :, :, w, :]
            r4, kk4 = (x[:, :, :].rearrange("p k (b t) -> p k b t", b=TB) for x in (r, kk))
            dve.do(lambda e: e.tensor_tensor(kk4, kk4, ld4, ALU.mult), a)
            for w, src in ((0, kk4), (1, None)):
                if w == 0:
                    for tb in range(TB):
                        dve.do(lambda e: e.tensor_scalar(ar[:, :, tb, 0, :], kk4[:, :, tb, :], -1.0, None, ALU.mult))
            a = act.do(lambda e: e.activation(t[:, :, :], dec[:, :, :], ACT.Exp), dve.last())
            for tb in range(TB):
                dve.do(lambda e: e.tensor_tensor(ar[:, :, tb, 1, :], r4[:, :, tb, :], t4[:, :, tb, :], ALU.mult), a)
            a = act.do(lambda e: e.activation(t[:, :, :], dec[:, :, :], ACT.Exp, scale=-1.0), dve.last())
            dve.do(lambda e: e.tensor_tensor(bt[:, :, :], bt[:, :, :], t[:, :, :], ALU.mult), a)
            dve.do(lambda e: e.tensor_tensor(kt[:, :, :], kt[:, :, :], t[:, :, :], ALU.mult))
            self.join()

    def rwkv_chunks(self, ctx, ar, bt, kt, v, y, carry):
        dve, act, pe = self.dve, self.act, self.pe
        sb = lambda name, shape, dt=F32: self.sb(ctx, "rc_" + name, shape, dt)
        c, cm = self.const(ctx, "gram_mask", "levels")
        dve.wait(*cm)
        G4 = HEADS // 4
        gram = sb("gram", [P, HEADS, 2, 2, P])
        inv, inv_t = sb("inv", [P, HEADS, P]), sb("inv_t", [P, HEADS, P])
        off, wt = sb("off", [P, HEADS, P]), sb("wt", [P, HEADS, P])
        z, u = sb("z", [P, HEADS, HD]), sb("u", [P, HEADS, HD])
        state = sb("state", [P, KT, HD])
        nat = off[:, :, :].rearrange("p (w k) c -> p w k c", w=2)
        mask = bcast(c["gram_mask"][:, :].rearrange("p (a t) -> p a t", a=2), 1, 2)
        for tb in range(TB):
            ts = slice(tb * P, (tb + 1) * P)
            grams = []
            for h in range(HEADS):
                r, j, b = slice((h % 2) * HD, (h % 2 + 1) * HD), h // 2, h % 8
                bank = self.banks[b]
                rhs = ar[r, j, tb, :, :].rearrange("p a t -> p (a t)")
                m = pe.run([lambda e, w=w, x=x: e.matmul(bank[:, w * SEQ:(w + 1) * SEQ], x[r, j, ts], rhs,
                                                         start=True, stop=True) for w, x in ((0, bt), (1, kt))],
                           *self.bank_free[b], act.last(), dve.last() if h == 0 else None)
                d = dve.do(lambda e: e.tensor_tensor(gram[:, h, :, :, :].rearrange("p w a t -> p w (a t)"),
                                                     bank[:, :].rearrange("p (w x) -> p w x", w=2),
                                                     bcast(c["gram_mask"][:, :], 1, 2), ALU.mult),
                           m, pe.last() if h == 0 else None, chain=False)
                self.bank_free[b] = (d,)
                grams.append(d)
            ring = Ring(list(range(8)))
            state_marks = [None] * G4
            ident = bcast(self.ident, 1, 4)
            for level in range(LEVELS):
                lm = bcast(c["levels"][:, level * P:(level + 1) * P], 1, 4)
                for q in range(G4):
                    hs = slice(4 * q, 4 * q + 4)
                    prev = state_marks[q]
                    wide = lambda bank: bank[:, :].rearrange("p (h t) -> p h t", h=4)
                    d = dve.do(lambda e: e.tensor_tensor(off[:, hs, :], gram[:, hs, 0, 0, :], lm, ALU.mult),
                               grams[4 * q + 3], pe.last(), chain=False)
                    b1 = self.banks[ring.take()[0]]
                    i1 = ring.at
                    if level == 0:
                        m = pe.run([lambda e, h=h: e.transpose(b1[:, (h % 4) * P:(h % 4 + 1) * P], off[:, h, :],
                                                               self.ident) for h in range(4 * q, 4 * q + 4)],
                                   d, *self.bank_free[i1])
                        d2 = dve.do(lambda e: e.tensor_tensor(inv_t[:, hs, :], off[:, hs, :], ident, ALU.add), d,
                                    chain=False)
                        d3 = dve.do(lambda e: e.tensor_tensor(inv[:, hs, :], wide(b1), ident, ALU.add), m,
                                    chain=False)
                        self.bank_free[i1] = (d3,)
                        state_marks[q] = (d2, d3)
                        continue
                    m = pe.run([lambda e, h=h: e.matmul(b1[:, (h % 4) * P:(h % 4 + 1) * P], off[:, h, :],
                                                        inv[:, h, :], start=True, stop=True)
                                for h in range(4 * q, 4 * q + 4)], d, *prev, *self.bank_free[i1])
                    a = act.do(lambda e: e.activation(wt[:, hs, :], wide(b1), ACT.Copy), m, pe.last(), chain=False)
                    self.bank_free[i1] = (a,)
                    b2 = self.banks[ring.take()[0]]
                    i2 = ring.at
                    m2 = pe.run([lambda e, h=h: e.matmul(b2[:, (h % 4) * P:(h % 4 + 1) * P], wt[:, h, :],
                                                         inv_t[:, h, :], start=True, stop=True)
                                 for h in range(4 * q, 4 * q + 4)], a, *self.bank_free[i2])
                    d3 = None
                    if level < LEVELS - 1:
                        b3 = self.banks[ring.take()[0]]
                        i3 = ring.at
                        m3 = pe.run([lambda e, h=h: e.matmul(b3[:, (h % 4) * P:(h % 4 + 1) * P], inv_t[:, h, :],
                                                             wt[:, h, :], start=True, stop=True)
                                     for h in range(4 * q, 4 * q + 4)], *self.bank_free[i3])
                        d3 = dve.do(lambda e: e.tensor_tensor(inv[:, hs, :], inv[:, hs, :], wide(b3), ALU.add), m3,
                                    chain=False)
                        self.bank_free[i3] = (d3,)
                    d2 = dve.do(lambda e: e.tensor_tensor(inv_t[:, hs, :], inv_t[:, hs, :], wide(b2), ALU.add),
                                m2, pe.last(), chain=False)
                    self.bank_free[i2] = (d2,)
                    state_marks[q] = (d2, d3)
            self.join()
            for b in range(8):
                self.bank_free[b] = ()

            def heads_product(banks, terms):
                makes = []
                for h in range(HEADS):
                    o = self.banks[banks[h % 2]][:, (h // 2) * HD:(h // 2 + 1) * HD]
                    ops = [t(h) for t in terms]
                    for i, (a, b) in enumerate(ops):
                        makes.append(lambda e, o=o, a=a, b=b, i=i, n=len(ops): e.matmul(
                            o, a, b, start=i == 0, stop=i == n - 1))
                return makes

            rows = lambda h: slice((h % 2) * HD, (h % 2 + 1) * HD)
            vh = lambda h: v[:, tb, h * HD:(h + 1) * HD]
            by_state = lambda w: [lambda h: (ar[rows(h), h // 2, tb, w, :], state[rows(h), h // 2, :])] if tb else []
            m = pe.run(heads_product((0, 1), [lambda h: (gram[:, h, 1, 0, :], vh(h))] + by_state(0)))
            z4 = z[:, :, :].rearrange("p (j e) i -> p j e i", e=2)
            u4 = u[:, :, :].rearrange("p (j e) i -> p j e i", e=2)
            y4 = y[:, tb, :].rearrange("p (j e i) -> p j e i", e=2, i=HD)
            for e_ in range(2):
                a = act.do(lambda e: e.activation(z4[:, :, e_, :], self.banks[e_][:, :].rearrange(
                    "p (j i) -> p j i", i=HD), ACT.Copy), m)
            m = pe.run(heads_product((2, 3), [lambda h: (inv_t[:, h, :], z[:, h, :])]), a)
            for e_ in range(2):
                a = act.do(lambda e: e.activation(u4[:, :, e_, :], self.banks[2 + e_][:, :].rearrange(
                    "p (j i) -> p j i", i=HD), ACT.Copy), m)
            m = pe.run(heads_product((4, 5), [lambda h: (gram[:, h, 1, 1, :], vh(h)),
                                              lambda h: (gram[:, h, 0, 1, :], u[:, h, :])] + by_state(1)), a)
            for e_ in range(2):
                a = act.do(lambda e: e.activation(y4[:, :, e_, :], self.banks[4 + e_][:, :].rearrange(
                    "p (j i) -> p j i", i=HD), ACT.Copy), m)
            if tb == 0:
                self.join()
                for w, x in ((0, bt), (1, kt)):
                    for n in range(2):
                        b = self.banks[2 * w + n]
                        m = pe.run([lambda e, i=i: e.transpose(b[:, i * P:(i + 1) * P], x[:, 4 * n + i, ts], self.ident)
                                    for i in range(4)])
                        a = act.do(lambda e: e.activation(nat[:, w, 4 * n:4 * n + 4, :],
                                                          b[:, :].rearrange("p (k c) -> p k c", k=4), ACT.Copy), m)
                makes = []
                for j in range(KT):
                    o = self.banks[4 + j // 4][:, (j % 4) * P:(j % 4 + 1) * P]
                    uj = u[:, 2 * j:2 * j + 2, :].rearrange("p h i -> p (h i)")
                    makes.append(lambda e, o=o, j=j, uj=uj: e.matmul(o, nat[:, 0, j, :], uj, start=True, stop=False))
                    makes.append(lambda e, o=o, j=j: e.matmul(o, nat[:, 1, j, :], v[:, tb, j * P:(j + 1) * P],
                                                              start=False, stop=True))
                m = pe.run(makes, a)
                for n in range(2):
                    for half in range(2):
                        r = slice(half * HD, (half + 1) * HD)
                        src = self.banks[4 + n][:, :].rearrange("p (k c) -> p k c", k=4)[r, :, half * HD:(half + 1) * HD]
                        dve.do(lambda e: e.tensor_tensor(state[r, 4 * n:4 * n + 4, :], src,
                                                         bcast(carry[r, 4 * n:4 * n + 4], 2, HD), ALU.mult), m)
            self.join()


STAGES = ["diff", "peer0", "stick", "peer1", "ffn00", "rwkv", "ffn01", "kv", "ffn10", "swa", "ffn11"]


def piece_list(dram, stages):
    out = []
    cols = lambda name, a, lo=0, hi=None: [(name, a[i]) for i in range(lo, hi if hi is not None else a.shape[0])]

    def rows(name, a, block=0):
        return [(name, a[k * P:(k + 1) * P, block * D:(block + 1) * D]) for k in range(KT)]

    for s in stages:
        if s == "diff":
            for b in range(3):
                out += rows("qkv", dram["w_qkv"], b)
            out += rows("w_o_a", dram["w_o_a"])
        elif s.startswith("peer"):
            layer = int(s[4])
            out += cols("pq", dram["peer_q"][layer])
            up = cols("u", dram["peer_u"][layer])
            down = [("v", dram["peer_v"][layer, i * P:(i + 1) * P, :]) for i in range(NKEY)]
            out.append(up[0])
            for i in range(NKEY):
                out += up[i + 1:i + 2] + [down[i]]
        elif s == "stick":
            out += cols("kv_k", dram["kv_k"]) + rows("kv_v", dram["w_kv"], 1) + cols("sb_q", dram["sb_q"])
            out += rows("w_o_b", dram["w_o_b"])
        elif s.startswith("ffn"):
            layer, which = int(s[3]), int(s[4])
            up = dram["ffn_in"][layer, which]
            down = dram["ffn_out"][layer, which]
            pair = lambda i: [("up", up[i]), ("up", up[FT + i])] if i < FT else []
            out += pair(0)
            for i in range(FT):
                out += pair(i + 1) + [("down", down[i * P:(i + 1) * P, :])]
        elif s == "rwkv":
            out += cols("rw_r", dram["rw_rk"], 0, 8) + cols("rw_k", dram["rw_rk"], 8, 16)
            out += rows("rw_v", dram["rw_v"]) + rows("rw_o", dram["rw_o"])
        elif s == "kv":
            out += cols("kv2_k", dram["kv2_k"]) + cols("kv2_v", dram["kv2_v"])
        elif s == "swa":
            out += cols("sw_q", dram["sw_q"]) + rows("sw_o", dram["sw_o"])
    return out


def build(nc, dram, out, stages=tuple(STAGES)):
    placed = {}
    with ExitStack() as ctx:
        go_through(Program(nc, dram, out, stages, ctx, placed))
        block = ctx.enter_context(nc.Block())

        @block.tensor
        def _(e):
            go_through(Program(nc, dram, out, stages, ctx, placed, "tensor", e))

        @block.scalar
        def _(e):
            go_through(Program(nc, dram, out, stages, ctx, placed, "scalar", e))

        @block.vector
        def _(e):
            go_through(Program(nc, dram, out, stages, ctx, placed, "vector", e))

        @block.gpsimd
        def _(e):
            go_through(Program(nc, dram, out, stages, ctx, placed, "gpsimd", e))

        @block.sync
        def _(e):
            go_through(Program(nc, dram, out, stages, ctx, placed, "sync", e))


def go_through(prog):
    prog.pieces = piece_list(prog.dram, prog.stages)
    prog.start()
    for s in prog.stages:
        if s == "diff":
            prog.diff()
        elif s.startswith("peer"):
            prog.peer(int(s[4]))
        elif s == "stick":
            prog.stick()
        elif s.startswith("ffn"):
            prog.ffn(int(s[3]), int(s[4]))
        elif s == "rwkv":
            prog.rwkv()
        elif s == "kv":
            prog.swa_kv()
        elif s == "swa":
            prog.swa()
    prog.finish()
    assert prog.used == len(prog.pieces)


def stationary_pieces(w):
    n = w.shape[-1]
    return w.reshape(KT, P, n // P, P).transpose(2, 1, 0, 3).reshape(n // P, P, D)


def lay_out(i):
    a = {k: np.asarray(v) for k, v in i.items()}
    ch = lambda v: np.asarray(v).reshape(-1, P).T
    pre = [a["norm_g_2"][l, s] for l in range(DEPTH) for s in (0, 2, 4)]
    kv2 = a["w_kv_2"]
    bk = a["b_kv_2"][:256].reshape(KV_HEADS, 1, HD)
    consts, fixed = constants()
    keys = a["peer_sub_keys"]
    kd = np.zeros((DEPTH, 2, HD, PH, 2, NKEY), np.float32)
    for c in range(2):
        kd[:, c, :, :, c, :] = keys[:, :, c].transpose(0, 3, 1, 2)
    rows = [a["ln_g"][l, s] if w == 0 else a["ln_b"][l, s] for l in range(2) for s in range(2) for w in range(2)]
    rows += [a["norm_g_2"][l, s] for l in range(2) for s in (1, 3, 5)]
    rows += [a["rwkv_gn_g_2"][0], a["rwkv_gn_b_2"][0], a["attn_b_o_2"][0]]
    return {
        "x": a["x"].reshape(SEQ, D), "consts": consts, "fixed": fixed,
        "chan": np.concatenate([ch(a["rwkv_mu_2"][0]), ch(a["rwkv_w0_2"][0]), ch(a["rwkv_a0_2"][0]),
                                ch(a["rwkv_k_k_2"][0]), ch(a["rwkv_k_a_2"][0]), ch(a["rwkv_r_k_2"][0]),
                                ch(np.stack(pre)), ch(a["kv_norm_g_2"]),
                                ch(np.broadcast_to(bk, (KV_HEADS, 2, HD))), ch(a["attn_b_q_2"][0])], axis=1),
        "small": np.concatenate([a["lambda_qk_a"][0].reshape(-1), a["subln_g_a"][0], a["attn_sinks_2"][0],
                                 a["b_kv_2"][256:]])[None],
        "rows": np.stack(rows),
        "keys": kd.reshape(DEPTH, P, PH, 2 * NKEY),
        "w_qkv": a["w_qkv_a"][0], "w_o_a": a["w_o_a"][0],
        "peer_q": np.stack([stationary_pieces(a["peer_w_q"][l]) for l in range(DEPTH)]),
        "peer_u": np.stack([stationary_pieces(a["peer_u"][l].T) for l in range(DEPTH)]),
        "peer_v": a["peer_v"],
        "kv_k": stationary_pieces(a["w_kv_b"][:, :D]), "w_kv": a["w_kv_b"],
        "sb_q": stationary_pieces(a["w_q_b"][0]), "w_o_b": a["w_o_b"][0],
        "ffn_in": np.stack([np.stack([stationary_pieces(a["ffn_w_in_2"][l, s]) for s in range(2)])
                            for l in range(DEPTH)]),
        "ffn_out": a["ffn_w_out_2"],
        "rw_rk": np.concatenate([stationary_pieces(a["rwkv_w_rkv_2"][0, 0]), stationary_pieces(a["rwkv_w_rkv_2"][0, 1])]),
        "rw_v": a["rwkv_w_rkv_2"][0, 2], "rw_o": a["rwkv_w_o_2"][0],
        "lora_w1": a["rwkv_w1_2"][0], "lora_w2": a["rwkv_w2_2"][0], "lora_a1": a["rwkv_a1_2"][0],
        "lora_a2": a["rwkv_a2_2"][0], "lora_g1": a["rwkv_g1_2"][0], "lora_g2": a["rwkv_g2_2"][0],
        "kv2_k": stationary_pieces(np.broadcast_to(kv2[:, :256].reshape(D, KV_HEADS, 1, HD),
                                                   (D, KV_HEADS, 2, HD)).reshape(D, 512)),
        "kv2_v": kv2[:, 256:].reshape(2, 4, P, 256).transpose(0, 2, 1, 3).reshape(2, P, D),
        "sw_q": stationary_pieces(a["attn_w_q_2"][0]), "sw_o": a["attn_w_o_2"][0],
    }


def kernel(**inputs):
    import concourse.bacc as bacc
    from concourse.bass_utils import run_bass_kernel_spmd

    nc = bacc.Bacc("TRN2", target_bir_lowering=False, num_devices=1)
    arrays = {f"in_{k}": np.ascontiguousarray(v) for k, v in lay_out(inputs).items()}
    dram = {k[3:]: nc.dram_tensor(k, v.shape, F32, kind="ExternalInput").ap() for k, v in arrays.items()}
    out = nc.dram_tensor("out", (SEQ, D), F32, kind="ExternalOutput").ap()
    build(nc, dram, out)
    r = run_bass_kernel_spmd(nc, [arrays], core_ids=[0])
    return r.results[0]["out"].reshape(1, SEQ, D)
```
